# Optimizing a Trainium2 kernel written in Bass

```python
import jax, jax.numpy as jnp
from jax import lax
import numpy as np

D_MODEL = 1024
BATCH = 1
SEQ = 2048
DEPTH = 1

CHUNK = 64
CONV_WIDTH = 3
D_CONV = D_MODEL
CONV_GROUPS = 16
HEAD_DIM = 64
N_Q_HEADS = 16
N_KV_HEADS = 2
GQA_GROUP = N_Q_HEADS // N_KV_HEADS
D_ATTN = N_Q_HEADS * HEAD_DIM
D_KV = N_KV_HEADS * HEAD_DIM
WINDOW = 128
WINDOW_CHUNKS = WINDOW // CHUNK
RMS_EPS = 1e-6
NEG_INF = -1e30

SPLIT_SIZES = (D_CONV, D_CONV, D_CONV, D_CONV,
               D_ATTN, D_KV, D_KV, D_ATTN,
               D_MODEL, D_MODEL)
SPLIT_POINTS = tuple(int(v) for v in np.cumsum(SPLIT_SIZES)[:-1])
D_IN_PROJ = int(sum(SPLIT_SIZES))

kernel_name = "hybrid_shortconv_swa_sink_gated_merge"

def rms_norm(x, g):
    xf = x.astype(jnp.float32)
    y = xf * lax.rsqrt(jnp.mean(xf * xf, axis=-1, keepdims=True) + RMS_EPS)
    return (y * g.astype(jnp.float32)).astype(x.dtype)

def causal_depthwise_conv(u, w):
    s = u.shape[1]
    up = jnp.pad(u, ((0, 0), (CONV_WIDTH - 1, 0), (0, 0)))
    out = w[CONV_WIDTH - 1] * up[:, CONV_WIDTH - 1:CONV_WIDTH - 1 + s]
    for j in range(CONV_WIDTH - 1):
        out = out + w[j] * up[:, j:j + s]
    return out

def window_blocks(t):
    n_chunks = t.shape[1]
    tp = jnp.pad(t, ((0, 0), (WINDOW_CHUNKS - 1, 0), (0, 0), (0, 0), (0, 0)))
    return jnp.concatenate([tp[:, j:j + n_chunks] for j in range(WINDOW_CHUNKS)], axis=2)

def sliding_window_attention_with_sinks(q, k, v, sinks):
    b, s, _ = q.shape
    n_chunks = s // CHUNK
    qc = q.reshape(b, n_chunks, CHUNK, N_KV_HEADS, GQA_GROUP, HEAD_DIM)
    kc = window_blocks(k.reshape(b, n_chunks, CHUNK, N_KV_HEADS, HEAD_DIM))
    vc = window_blocks(v.reshape(b, n_chunks, CHUNK, N_KV_HEADS, HEAD_DIM))
    scale = HEAD_DIM ** -0.5
    scores = jnp.einsum('bcqhgd,bckhd->bchgqk', qc, kc).astype(jnp.float32) * scale
    chunk_idx = jnp.arange(n_chunks)[:, None]
    key_block = jnp.arange(WINDOW_CHUNKS * CHUNK)[None, :] // CHUNK
    valid = (chunk_idx + key_block - (WINDOW_CHUNKS - 1)) >= 0
    scores = jnp.where(valid[None, :, None, None, None, :], scores, NEG_INF)
    sink = sinks.astype(jnp.float32).reshape(N_KV_HEADS, GQA_GROUP)[None, None, :, :, None, None]
    m = jnp.maximum(jnp.max(scores, axis=-1, keepdims=True), sink)
    p = jnp.exp(scores - m)
    probs = p / (jnp.sum(p, axis=-1, keepdims=True) + jnp.exp(sink - m))
    o = jnp.einsum('bchgqk,bckhd->bcqhgd', probs.astype(v.dtype), vc)
    return o.reshape(b, s, D_ATTN)

def setup_inputs(seed: int = 0) -> dict:
    key = jax.random.key(seed)
    ks = jax.random.split(key, 10)
    x = jax.random.normal(ks[0], (BATCH, SEQ, D_MODEL), jnp.float32)
    norm_pre = 1.0 + 0.05 * jax.random.normal(ks[1], (DEPTH, D_MODEL), jnp.float32)
    w_in = jax.random.normal(ks[2], (DEPTH, D_MODEL, D_IN_PROJ), jnp.float32) * D_MODEL ** -0.5
    conv_w = jax.random.normal(ks[3], (DEPTH, CONV_WIDTH, D_CONV), jnp.float32) * CONV_WIDTH ** -0.5
    sinks = 0.5 * jax.random.normal(ks[4], (DEPTH, N_Q_HEADS), jnp.float32)
    w_proj_a = jax.random.normal(ks[5], (DEPTH, D_CONV, D_MODEL), jnp.float32) * D_CONV ** -0.5
    w_proj_b = jax.random.normal(ks[6], (DEPTH, D_ATTN, D_MODEL), jnp.float32) * D_ATTN ** -0.5
    w_out = jax.random.normal(ks[7], (DEPTH, D_MODEL, D_MODEL), jnp.float32) * D_MODEL ** -0.5
    norm_post = 1.0 + 0.05 * jax.random.normal(ks[8], (DEPTH, D_MODEL), jnp.float32)
    return {"x": x, "norm_pre": norm_pre, "w_in": w_in, "conv_w": conv_w, "sinks": sinks,
            "w_proj_a": w_proj_a, "w_proj_b": w_proj_b, "w_out": w_out, "norm_post": norm_post}

def reference(x, norm_pre, w_in, conv_w, sinks, w_proj_a, w_proj_b, w_out, norm_post):
    for i in range(DEPTH):
        h = rms_norm(x, norm_pre[i])
        proj = jnp.einsum('bsd,de->bse', h, w_in[i])
        xa, b_gate, c_gate, z_a, q, k, v, z_b, g_a, g_b = jnp.split(proj, SPLIT_POINTS, axis=-1)
        u_a = b_gate * causal_depthwise_conv(c_gate * xa, conv_w[i]) * jax.nn.silu(z_a)
        y_a = jnp.einsum('bsc,cd->bsd', u_a, w_proj_a[i])
        u_b = sliding_window_attention_with_sinks(q, k, v, sinks[i]) * jax.nn.silu(z_b)
        y_b = jnp.einsum('bsc,cd->bsd', u_b, w_proj_b[i])
        merged = jax.nn.sigmoid(g_a) * y_a + jax.nn.sigmoid(g_b) * y_b
        out = jnp.einsum('bsd,de->bse', merged, w_out[i])
        x = x + rms_norm(out, norm_post[i])
    return x


_drawn_inputs = setup_inputs


def setup_inputs(seed=0):
    import zlib

    import numpy as np

    out = dict(_drawn_inputs(seed))
    spreads = {}
    factors = {'sinks': 8.0}
    for name, (base, spread) in spreads.items():
        noise = np.random.default_rng([zlib.crc32(name.encode()), seed]).standard_normal(out[name].shape)
        drawn = base * np.exp(spread * noise) if base else spread * noise
        out[name] = __import__('jax').numpy.asarray(drawn.astype(out[name].dtype))
    for name, factor in factors.items():
        out[name] = (out[name] * factor).astype(out[name].dtype)
    return out
```

```python
import concourse.bass as bass
from concourse import mybir
from contextlib import ExitStack


def hybrid_trunk(nc, x, norm_pre, w_in, conv_w, sinks, w_proj_a, w_proj_b, w_out, norm_post, out):
    f32, f32r = mybir.dt.float32, mybir.dt.float32r
    ACT, ALU, AX = mybir.ActivationFunctionType, mybir.AluOpType, mybir.AxisListType

    P = 128
    _, S, D = x.shape
    KT = D // P
    TB = 512
    NB = S // TB
    NT = TB // P
    CHUNK, HD = 64, 64
    NC = TB // CHUNK
    UNIT = 4
    NU = NC // UNIT
    NH = sinks.shape[1]
    NPAIR = NH // 2
    CW = conv_w.shape[1]
    DKV = (w_in.shape[2] - 8 * D) // 2
    SCALE = HD ** -0.5
    EPS = 1e-6
    NEG = -1e30
    assert DKV == P and CW == 3 and NPAIR * HD * 2 == D

    C_XA, C_B, C_C, C_ZA, C_Q = 0, D, 2 * D, 3 * D, 4 * D
    C_K = 5 * D
    C_V = C_K + DKV
    C_ZB = C_V + DKV
    C_GA = C_ZB + D
    C_GB = C_GA + D

    J_CONV = 0
    J_CA = J_CONV + 4 * KT
    J_KV = J_CA + 2 * KT
    J_AT = J_KV + 2
    J_CB = J_AT + 2 * NPAIR
    J_FIN = J_CB + 2 * KT
    NJ = J_FIN + KT
    U_CONV, U_CA, U_KV = 0, KT, 2 * KT
    U_AT = U_KV + 1
    U_CB = U_AT + NPAIR
    U_FIN = U_CB + KT
    NU01 = U_FIN + KT // 2

    win = w_in[0].rearrange("(t p) n -> p t n", p=P)
    wpa = w_proj_a[0].rearrange("(t p) n -> p t n", p=P)
    wpb = w_proj_b[0].rearrange("(g j d) n -> g d j n", g=2, d=HD)
    wo = w_out[0].rearrange("(t p) n -> p t n", p=P)
    x_tiles = x.rearrange("a (t p) d -> (a t) p d", p=P)
    out_tiles = out.rearrange("a (t p) d -> (a t) p d", p=P)

    with ExitStack() as ctx:
        def sb(name, shape, dt=f32):
            return ctx.enter_context(nc.sbuf_tensor(name, shape, dt))

        def sem(name):
            return ctx.enter_context(nc.semaphore(name))

        h_hi, h_lo = sb("h_hi", [P, KT, TB], f32r), sb("h_lo", [P, KT, TB], f32r)
        u_hi, u_lo = sb("u_hi", [P, KT, TB], f32r), sb("u_lo", [P, KT, TB], f32r)
        m_hi, m_lo = sb("m_hi", [P, KT, TB], f32r), sb("m_lo", [P, KT, TB], f32r)
        m_a = sb("m_a", [P, KT, TB])
        xn = m_a[:, :, :].rearrange("p k n -> p (k n)").rearrange("p (t d) -> p t d", t=NT)
        w_raw = sb("w_raw", [P, 2, KT, P])
        w_hi, w_lo = sb("w_hi", [P, 2, KT, P], f32r), sb("w_lo", [P, 2, KT, P], f32r)
        work = sb("work", [P, KT, TB])
        xa_s, th, sg, v_s, t_a, t_b, u_f = (work[:, n, :] for n in range(7))
        p_s = [work[:, 4, :], work[:, 5, :]]
        cx = sb("cx", [P, CW - 1 + TB])
        cx_tail = sb("cx_tail", [P, KT, CW - 1])
        k_hi, k_lo = sb("k_hi", [P, CHUNK + TB], f32r), sb("k_lo", [P, CHUNK + TB], f32r)
        v_t = sb("v_t", [P, CHUNK + TB])
        v_hi, v_lo = sb("v_hi", [P, NC, P], f32r), sb("v_lo", [P, NC, P], f32r)
        q_hi, q_lo = sb("q_hi", [P, NC, P], f32r), sb("q_lo", [P, NC, P], f32r)
        pt_hi, pt_lo = sb("pt_hi", [P, NU, TB], f32r), sb("pt_lo", [P, NU, TB], f32r)
        xt = sb("xt", [P, 4, D])
        ident = sb("ident", [P, P])
        gpost = sb("gpost", [P, D])
        gpre = sb("gpre", [P, KT])
        taps = sb("taps", [P, CW, KT])
        sink = sb("sink", [P, NPAIR])
        nsink = sb("nsink", [P, NPAIR])
        mask0 = sb("mask0", [P, 1])
        mx = sb("mx", [P, NU, UNIT])
        negm = sb("negm", [P, NU, UNIT])
        esum = sb("esum", [P, NU, UNIT])
        esink = sb("esink", [P, NU, UNIT])
        den = sb("den", [P, NU, UNIT])
        rden = sb("rden", [P, NU, UNIT])
        ssx = sb("ssx", [P, NT])
        msx = sb("msx", [P, NT])
        rsx = sb("rsx", [P, NT])
        sso = sb("sso", [P, NT])
        mso = sb("mso", [P, NT])
        rso = sb("rso", [P, NT])
        mhalf, inv_d, eps = sb("mhalf", [P, NT]), sb("inv_d", [P, NT]), sb("eps", [P, NT])

        bank = [ctx.enter_context(nc.psum_tensor(f"bank{n}", [P, TB], f32)) for n in range(2)]
        bank23 = ctx.enter_context(nc.psum_tensor("bank23", [P, 2, TB], f32))
        aux = ctx.enter_context(nc.psum_tensor("aux", [P, 4, TB], f32))
        bank += [bank23[:, 0, :], bank23[:, 1, :]]

        raw_loaded = [sem(f"raw_loaded{n}") for n in range(2)]
        whi_ready, wlo_ready = sem("whi_ready"), sem("wlo_ready")
        job_done = sem("job_done")
        drained = [sem(f"drained{n}") for n in range(3)]
        consts_loaded, consts_made = sem("consts_loaded"), sem("consts_made")
        pool_set, ident_ready = sem("pool_set"), sem("ident_ready")
        x_loaded = [sem(f"x_loaded{n}") for n in range(NT)]
        res_loaded = [sem(f"res_loaded{n}") for n in range(NT)]
        stored = [sem(f"stored{n}") for n in range(NT)]
        xsq_done, xms_done, xrs_ready, xn_ready = map(sem, ("xsq_done", "xms_done", "xrs_ready", "xn_ready"))
        xT_done, hhi_ready, hlo_ready = map(sem, ("xT_done", "hhi_ready", "hlo_ready"))
        tap2_done, tap1_done, tap0_done = map(sem, ("tap2_done", "tap1_done", "tap0_done"))
        tanh_ready, gate_ready, bgate_ready = map(sem, ("tanh_ready", "gate_ready", "bgate_ready"))
        uf_ready, uhi_ready, ulo_ready = map(sem, ("uf_ready", "uhi_ready", "ulo_ready"))
        kvhead_ready, khi_ready, vT_done, vhi_ready, vlo_ready = map(
            sem, ("kvhead_ready", "khi_ready", "vT_done", "vhi_ready", "vlo_ready"))
        tails_moved, klo_tail_moved = sem("tails_moved"), sem("klo_tail_moved")
        qhi_ready = sem("qhi_ready")
        scores_done, masked, max_ready, negm_ready, exp_done = map(
            sem, ("scores_done", "masked", "max_ready", "negm_ready", "exp_done"))
        den_ready, rden_ready, probs_ready = map(sem, ("den_ready", "rden_ready", "probs_ready"))
        pT_done, pthi_ready, ptlo_ready, pv_done = map(sem, ("pT_done", "pthi_ready", "ptlo_ready", "pv_done"))
        mf_ready, msum_ready, mhi_ready, mlo_ready = map(sem, ("mf_ready", "msum_ready", "mhi_ready", "mlo_ready"))
        oT_done, osq_done, oms_done, ors_ready, y_ready, res_added = map(
            sem, ("oT_done", "osq_done", "oms_done", "ors_ready", "y_ready", "res_added"))

        def f(ap):
            return ap.bitcast(f32)

        def blocks(eng, body):
            with eng.Fori(0, NB - 1) as b:
                body(b, False)
            body(NB - 1, True)

        block = ctx.enter_context(nc.Block())

        @block.sync
        def _(sp):
            def load(slot, parts):
                for dst, src in parts:
                    sp.dma_start(dst, src).then_inc(raw_loaded[slot], 16)

            def cols(slot, src, at):
                h = KT // 2
                return [(w_raw[:, slot, k * h:(k + 1) * h, :], src[:, k * h:(k + 1) * h, bass.ds(at, P)])
                        for k in (1, 0)]

            def head_cols(slot, base, j):
                return [(w_raw[:, slot, :, g * HD:(g + 1) * HD],
                         win[:, :, bass.ds(j * HD + base + g * NPAIR * HD, HD)]) for g in range(2)]

            def head_rows(slot, at):
                return [(w_raw[g * HD:(g + 1) * HD, slot, :, :], wpb[g][:, :, bass.ds(at, P)])
                        for g in (1, 0)]

            def rows(tiles, b, t):
                return tiles[b * NT + t] if isinstance(b, int) else tiles[bass.ds(b * NT + t, 1)].squeeze(0)

            def column(at):
                return at if isinstance(at, int) else sp.snap(at)

            def slot_free(b, j):
                sp.wait_ge(wlo_ready, b * NJ + j - 1)

            def x_rows(b):
                for t in range(NT):
                    sp.dma_start(xt[:, t, :], rows(x_tiles, b, t)).then_inc(x_loaded[t], 16)

            def residual(b, t):
                sp.dma_start(xt[:, t, :], rows(x_tiles, b, t)).then_inc(res_loaded[t], 16)

            def conv(b, i, s0, s1, first=False):
                for s in range(s0, s1):
                    at = column(i * P + (C_XA, C_C, C_ZA, C_B)[s])
                    if not first:
                        slot_free(b, i * 4 + s)
                    load(s % 2, cols(s % 2, win, at))

            x_rows(0)
            conv(0, 0, 0, 2, first=True)
            conv(0, 0, 2, 4)

            def body(b, last):
                with sp.Fori(1, KT) as i:
                    conv(b, i, 0, 4)
                with sp.Fori(0, KT) as i:
                    for s, (src, c) in enumerate(((win, C_GA), (wpa, 0))):
                        at = column(i * P + c)
                        slot_free(b, i * 2 + J_CA + s)
                        load(s, cols(s, src, at))
                for s, c in enumerate((C_K, C_V)):
                    slot_free(b, J_KV + s)
                    load(s, cols(s, win, c))
                with sp.Fori(0, NPAIR) as j:
                    for s, c in enumerate((C_Q, C_ZB)):
                        slot_free(b, j * 2 + J_AT + s)
                        load(s, head_cols(s, c, j))
                if not last:
                    x_rows(b + 1)
                with sp.Fori(0, KT) as i:
                    gates, rows_b = column(i * P + C_GB), column(i * P)
                    slot_free(b, i * 2 + J_CB)
                    load(0, cols(0, win, gates))
                    slot_free(b, i * 2 + J_CB + 1)
                    load(1, head_rows(1, rows_b))
                with sp.Fori(0, KT // 2) as i:
                    for s in range(2):
                        at = column(i * 2 * P + s * P)
                        slot_free(b, i * 2 + J_FIN + s)
                        load(s, cols(s, wo, at))

                for t in range(NT):
                    if not last:
                        sp.wait_ge(xn_ready, b * NT + NT + t + 1)
                    residual(b, t)
                if not last:
                    conv(b + 1, 0, 0, 2)
                for t in range(NT):
                    sp.wait_ge(res_added, b * NT + t + 1)
                    sp.dma_start(rows(out_tiles, b, t), xt[:, t, :]).then_inc(stored[t], 16)
                if not last:
                    conv(b + 1, 0, 2, 3)
                    all_stored = sp.snap(b * 16 + 16)
                    slot_free(b + 1, 3)
                    for t in range(NT):
                        sp.wait_ge(stored[t], all_stored)
                    load(1, cols(1, win, C_B))
                else:
                    for t in range(NT):
                        sp.wait_ge(stored[t], b * 16 + 16)

            blocks(sp, body)

        @block.tensor
        def _(pe):
            def job(b, j, slot, bk, use, hi, lo, tail=None):
                pe.wait_ge(wlo_ready, b * NJ + j + 1)
                if bk < 2:
                    pe.wait_ge(drained[bk], b * NU01 + use + 1)
                elif bk == 2:
                    pe.wait_ge(drained[2], b * KT + use + 1)
                else:
                    pe.wait_ge(uf_ready, b * 2 * KT + use + 1)
                for k in range(KT):
                    if k == KT - 1 and tail:
                        tail()
                    for n, (w, a) in enumerate(((w_hi, hi), (w_hi, lo), (w_lo, hi))):
                        mm = nc.tensor.matmul(bank[bk][:, :], w[:, slot, k, :], a[:, k, :],
                                              start=(k == 0 and n == 0), stop=(k == KT - 1 and n == 2))
                mm.then_inc(job_done, 1)

            def norm_transposes(b, i):
                pe.wait_ge(xn_ready, b * NT + NT)
                if not (isinstance(b, int) and i == 0):
                    pe.wait_ge(hlo_ready, b * KT + i * 2)
                for s in range(2):
                    for t in range(NT):
                        mm = nc.tensor.transpose(aux[:, s, t * P:(t + 1) * P],
                                                 xn[:, t, (i * 2 + s) * P:(i * 2 + s + 1) * P], ident[:, :])
                    mm.then_inc(xT_done, 1)

            def probs_transposes(b, j):
                for u in range(NU):
                    pe.wait_ge(probs_ready, (b * NPAIR + j) * NU + u + 1)
                    for c in range(UNIT):
                        mm = nc.tensor.transpose(aux[:, 2 + u, c * P:(c + 1) * P],
                                                 p_s[u][:, c * P:(c + 1) * P], ident[:, :])
                    mm.then_inc(pT_done, 1)

            def scores(b, j):
                pe.wait_ge(drained[0], b * NU01 + j + U_AT + 2)
                for u in range(NU):
                    for c in range(UNIT):
                        n = u * UNIT + c
                        k0 = n * CHUNK
                        for m, (q, k) in enumerate(((q_hi, k_hi), (q_hi, k_lo), (q_lo, k_hi))):
                            mm = nc.tensor.matmul(aux[:, u, c * P:(c + 1) * P], q[:, n, :],
                                                  k[:, k0:k0 + 2 * CHUNK], start=(m == 0), stop=(m == 2))
                    mm.then_inc(scores_done, 1)

            def values(b, j):
                pe.wait_ge(ptlo_ready, (b * NPAIR + j) * NU + NU)
                pe.wait_ge(uf_ready, b * 2 * KT + KT + j + 1)
                for u in range(NU):
                    for c in range(UNIT):
                        n = u * UNIT + c
                        for m, (v, pt) in enumerate(((v_hi, pt_hi), (v_hi, pt_lo), (v_lo, pt_hi))):
                            mm = nc.tensor.matmul(bank23[:, u, c * P:(c + 1) * P], v[:, n, :],
                                                  pt[:, u, c * P:(c + 1) * P], start=(m == 0), stop=(m == 2))
                mm.then_inc(pv_done, 1)

            pe.wait_ge(ident_ready, 1)
            for i in range(KT // 2):
                norm_transposes(0, i)

            def body(b, last):
                with pe.Fori(0, KT) as i:
                    pe.wait_ge(hlo_ready, b * KT + KT)
                    for s in range(4):
                        job(b, i * 4 + s, s % 2, s, i + U_CONV, h_hi, h_lo)
                with pe.Fori(0, KT) as i:
                    job(b, i * 2 + J_CA, 0, 0, i + U_CA, h_hi, h_lo)
                    pe.wait_ge(ulo_ready, b * 2 * KT + KT)
                    job(b, i * 2 + J_CA + 1, 1, 1, i + U_CA, u_hi, u_lo)
                job(b, J_KV, 0, 0, U_KV, h_hi, h_lo)
                job(b, J_KV + 1, 1, 1, U_KV, h_hi, h_lo)
                job(b, J_AT, 0, 0, U_AT, h_hi, h_lo)
                pe.wait_ge(drained[1], b * NU01 + U_KV + 2)
                for u in range(NU):
                    for c in range(UNIT):
                        k0 = (u * UNIT + c) * CHUNK
                        mm = nc.tensor.transpose(aux[:, u, c * P:(c + 1) * P], v_t[:, k0:k0 + 2 * CHUNK], ident[:, :])
                    mm.then_inc(vT_done, 1)
                job(b, J_AT + 1, 1, 1, U_AT, h_hi, h_lo)
                pe.wait_ge(vlo_ready, b * NU + NU)
                scores(b, 0)
                with pe.Fori(1, NPAIR) as j:
                    job(b, j * 2 + J_AT, 0, 0, j + U_AT, h_hi, h_lo)
                    probs_transposes(b, j - 1)
                    job(b, j * 2 + J_AT + 1, 1, 1, j + U_AT, h_hi, h_lo)
                    scores(b, j)
                    values(b, j - 1)
                job(b, J_CB, 0, 0, U_CB, h_hi, h_lo)
                probs_transposes(b, NPAIR - 1)
                values(b, NPAIR - 1)
                job(b, J_CB + 1, 1, 1, U_CB, u_hi, u_lo,
                    tail=lambda: pe.wait_ge(ulo_ready, b * 2 * KT + KT + NPAIR))
                with pe.Fori(1, KT) as i:
                    job(b, i * 2 + J_CB, 0, 0, i + U_CB, h_hi, h_lo)
                    job(b, i * 2 + J_CB + 1, 1, 1, i + U_CB, u_hi, u_lo)
                pe.wait_ge(mlo_ready, b * KT + KT)

                def final(i):
                    job(b, i * 2 + J_FIN, 0, 0, i + U_FIN, m_hi, m_lo)
                    job(b, i * 2 + J_FIN + 1, 1, 1, i + U_FIN, m_hi, m_lo)

                if last:
                    with pe.Fori(0, KT // 2) as i:
                        final(i)
                else:
                    for i in range(KT // 2):
                        final(i)
                        norm_transposes(b + 1, i)
                for bk in range(2):
                    pe.wait_ge(drained[bk], b * NU01 + NU01 + 1)
                if not last:
                    pe.wait_ge(hlo_ready, b * KT + 2 * KT)
                for t in range(NT):
                    if t >= 2:
                        pe.wait_ge(res_added, b * NT + t - 1)
                    for k in range(KT):
                        a = 2 * (t % 2) + k // 4
                        mm = nc.tensor.transpose(aux[:, a, k % 4 * P:(k % 4 + 1) * P],
                                                 work[:, k, t * P:(t + 1) * P], ident[:, :])
                    mm.then_inc(oT_done, 1)
                pe.wait_ge(res_added, b * NT + NT)

            blocks(pe, body)

        @block.scalar
        def _(act):
            def split_hi(b, j, slot, ahead=2):
                n = j + ahead
                act.wait_ge(raw_loaded[slot], b * (NJ * 16) + (n - slot) * 16 + 32)
                if ahead:
                    act.wait_ge(job_done, b * NJ + j + 1)
                nc.scalar.activation(w_hi[:, slot], w_raw[:, slot], ACT.Copy).then_inc(whi_ready, 1)

            def row_squares(b, first=False):
                if not first:
                    act.wait_ge(mlo_ready, b * KT)
                for t in range(NT):
                    act.wait_ge(x_loaded[t], b * 16 + 16)
                    nc.scalar.activation(xn[:, t, :], xt[:, t, :], ACT.Square,
                                         accum_out=ssx[:, t:t + 1]).then_inc(xsq_done, 1)

            def norm_hi(b, i):
                for s in range(2):
                    act.wait_ge(xT_done, b * KT + i * 2 + s + 1)
                    nc.scalar.activation(h_hi[:, bass.ds(i * 2 + s, 1), :], aux[:, s:s + 1, :], ACT.Copy,
                                         scale=gpre[:, bass.ds(i * 2 + s, 1)]).then_inc(hhi_ready, 1)

            def probs_hi(b, j):
                for u in range(NU):
                    act.wait_ge(pT_done, (b * NPAIR + j) * NU + u + 1)
                    nc.scalar.activation(pt_hi[:, u, :], aux[:, 2 + u, :], ACT.Copy).then_inc(pthi_ready, 1)

            def u_high(b, n, k):
                act.wait_ge(uf_ready, b * 2 * KT + n + 2)
                nc.scalar.activation(u_hi[:, k, :] if isinstance(k, int) else u_hi[:, bass.ds(k, 1), :].squeeze(1),
                                     u_f, ACT.Copy, scale=0.5).then_inc(uhi_ready, 1)

            def exps(b, j, jcol):
                for u in range(NU):
                    act.wait_ge(negm_ready, (b * NPAIR + j) * NU + u + 1)
                    for c in range(UNIT):
                        nc.scalar.activation(p_s[u][:, c * P:(c + 1) * P], aux[:, u, c * P:(c + 1) * P], ACT.Exp,
                                             bias=negm[:, u, c:c + 1], scale=SCALE, accum_out=esum[:, u, c:c + 1])
                    nc.scalar.activation(esink[:, u, :], negm[:, u, :], ACT.Exp,
                                         bias=jcol).then_inc(exp_done, 1)

            with nc.allow_non_contiguous_dma(reason="small constants, once"):
                act.dma_start(gpre[:, :], norm_pre[0].rearrange("(t p) -> p t", p=P)).then_inc(consts_loaded, 16)
                for w in range(CW):
                    act.dma_start(taps[:, w, :], conv_w[0, w].rearrange("(t p) -> p t", p=P)).then_inc(consts_loaded, 16)
            act.dma_start(gpost[:, :], norm_post[0:1, :].to_broadcast([P, D])).then_inc(consts_loaded, 16)
            for g in range(2):
                act.dma_start(sink[g * HD:(g + 1) * HD, :],
                             sinks[0:1, g * NPAIR:(g + 1) * NPAIR].to_broadcast([HD, NPAIR])).then_inc(consts_loaded, 16)
            act.wait_ge(consts_loaded, 16 * (CW + 4))
            row_squares(0, first=True)
            for s in range(2):
                split_hi(0, s, s, ahead=0)
            with act.Fori(0, KT // 2) as i:
                norm_hi(0, i)

            def body(b, last):
                with act.Fori(0, KT) as i:
                    j = i * 4
                    split_hi(b, j, 0)
                    act.wait_ge(drained[1], b * NU01 + i + 1)
                    nc.scalar.activation(xa_s, bank[0][:, :], ACT.Copy).then_inc(drained[0], 1)
                    split_hi(b, j + 1, 1)
                    split_hi(b, j + 2, 0)
                    act.wait_ge(drained[2], b * KT + i + 1)
                    nc.scalar.activation(th, bank[2][:, :], ACT.Tanh, scale=0.5).then_inc(tanh_ready, 1)
                    split_hi(b, j + 3, 1)
                    u_high(b, i, i)
                with act.Fori(0, KT) as i:
                    j = i * 2 + J_CA
                    split_hi(b, j, 0)
                    act.wait_ge(drained[1], b * NU01 + i + U_CA + 1)
                    nc.scalar.activation(th, bank[0][:, :], ACT.Tanh, scale=0.5).then_inc(drained[0], 1)
                    split_hi(b, j + 1, 1)
                act.wait_ge(kvhead_ready, 1)
                nc.scalar.activation(k_hi[:, 0:CHUNK], f(k_hi[:, TB:TB + CHUNK]), ACT.Copy)
                nc.scalar.activation(v_t[:, 0:CHUNK], v_t[:, TB:TB + CHUNK], ACT.Copy).then_inc(tails_moved, 1)
                split_hi(b, J_KV, 0)
                act.wait_ge(tails_moved, b + 1)
                nc.scalar.activation(k_hi[:, CHUNK:], bank[0][:, :], ACT.Copy).then_inc(khi_ready, 1)
                split_hi(b, J_KV + 1, 1)
                nc.scalar.activation(v_t[:, CHUNK:], bank[1][:, :], ACT.Copy).then_inc(drained[1], 1)

                def q_high(j):
                    act.wait_ge(job_done, b * NJ + j * 2 + J_AT + 1)
                    q = bank[0][:, :].rearrange("p (c n) -> p c n", n=CHUNK)
                    for g in range(2):
                        r = slice(g * HD, (g + 1) * HD)
                        i_ = nc.scalar.activation(q_hi[r, :, g * CHUNK:(g + 1) * CHUNK], q[r], ACT.Copy)
                    i_.then_inc(qhi_ready, 1)

                def z_tanh():
                    nc.scalar.activation(th, bank[1][:, :], ACT.Tanh, scale=0.5).then_inc(tanh_ready, 1)

                split_hi(b, J_AT, 0)
                q_high(0)
                for u in range(NU):
                    act.wait_ge(vT_done, b * NU + u + 1)
                    nc.scalar.activation(v_hi[:, u * UNIT:(u + 1) * UNIT, :].rearrange("p c n -> p (c n)"),
                                         aux[:, u, :], ACT.Copy).then_inc(vhi_ready, 1)
                split_hi(b, J_AT + 1, 1)
                z_tanh()
                exps(b, 0, sink[:, 0:1])
                with act.Fori(1, NPAIR) as j:
                    split_hi(b, j * 2 + J_AT, 0)
                    q_high(j)
                    probs_hi(b, j - 1)
                    split_hi(b, j * 2 + J_AT + 1, 1)
                    act.wait_ge(drained[1], b * NU01 + j + U_AT + 1)
                    z_tanh()
                    exps(b, j, sink[:, bass.ds(j, 1)])
                    u_high(b, j + (KT - 1), j - 1)
                split_hi(b, J_CB, 0)
                act.wait_ge(drained[1], b * NU01 + U_CB + 1)
                nc.scalar.activation(th, bank[0][:, :], ACT.Tanh, scale=0.5).then_inc(drained[0], 1)
                probs_hi(b, NPAIR - 1)
                u_high(b, KT + NPAIR - 1, NPAIR - 1)

                def m_high(i):
                    act.wait_ge(msum_ready, b * KT + i + 1)
                    k = m_hi[:, 0, :] if isinstance(i, int) else m_hi[:, bass.ds(i, 1), :].squeeze(1)
                    nc.scalar.activation(k, u_f, ACT.Copy, scale=0.5).then_inc(mhi_ready, 1)

                split_hi(b, J_CB + 1, 1)
                m_high(0)
                with act.Fori(1, KT) as i:
                    j = i * 2 + J_CB
                    split_hi(b, j, 0)
                    act.wait_ge(drained[1], b * NU01 + i + U_CB + 1)
                    nc.scalar.activation(th, bank[0][:, :], ACT.Tanh, scale=0.5).then_inc(drained[0], 1)
                    split_hi(b, j + 1, 1)
                    m_high(i)

                if not last:
                    row_squares(b + 1)

                def final(i, split=True):
                    j = i * 2 + J_FIN
                    if split:
                        split_hi(b, j, 0)
                    act.wait_ge(job_done, b * NJ + j + 1)
                    o = work[:, bass.ds(i * 2, 1), :].squeeze(1) if not isinstance(i, int) else work[:, i * 2, :]
                    nc.scalar.activation(o, bank[0][:, :], ACT.Copy).then_inc(drained[0], 1)
                    if split:
                        split_hi(b, j + 1, 1)
                    if not last:
                        norm_hi(b + 1, i)

                if last:
                    with act.Fori(0, KT // 2 - 1) as i:
                        final(i)
                    final(KT // 2 - 1, split=False)
                else:
                    with act.Fori(0, KT // 2) as i:
                        final(i)
                for t in range(NT):
                    act.wait_ge(oT_done, b * NT + t + 1)
                    a = 2 * (t % 2)
                    nc.scalar.activation(m_lo[:, 2 * t:2 * t + 2, :], aux[:, a:a + 2, :], ACT.Square,
                                         accum_out=sso[:, t:t + 1]).then_inc(osq_done, 1)

            blocks(act, body)

        @block.vector
        def _(dve):
            V = nc.vector

            def split_lo(b, j, slot, ahead=2):
                n = j + ahead
                dve.wait_ge(whi_ready, b * NJ + n + 1)
                V.tensor_tensor(w_lo[:, slot], w_raw[:, slot], f(w_hi[:, slot]), ALU.subtract).then_inc(wlo_ready, 1)

            def row_scale(b):
                dve.wait_ge(xrs_ready, b + 1)
                for t in range(NT):
                    V.tensor_scalar(xn[:, t, :], xt[:, t, :], rsx[:, t:t + 1], None, ALU.mult).then_inc(xn_ready, 1)

            def at(tensor, i, step=1, off=0):
                return tensor[:, i * step + off, :] if isinstance(i, int) else tensor[:, bass.ds(i * step + off, 1), :].squeeze(1)

            def norm_lo(b, i):
                for s in range(2):
                    dve.wait_ge(hhi_ready, b * KT + i * 2 + s + 1)
                    k = i * 2 + s
                    V.scalar_tensor_tensor(h_lo[:, bass.ds(k, 1), :], aux[:, s:s + 1, :], gpre[:, bass.ds(k, 1)],
                                           f(h_hi[:, bass.ds(k, 1), :]), ALU.mult, ALU.subtract).then_inc(hlo_ready, 1)

            def u_low(b, n, k):
                dve.wait_ge(uhi_ready, b * 2 * KT + n + 1)
                V.scalar_tensor_tensor(at(u_lo, k), u_f, 0.5, f(at(u_hi, k)), ALU.mult,
                                       ALU.subtract).then_inc(ulo_ready, 1)

            V.memset(cx_tail[:, :, :], 0.0).then_inc(drained[0], 1)
            V.memset(k_hi[:, TB:TB + CHUNK].bitcast(mybir.dt.uint32), 0).then_inc(drained[1], 1)
            V.memset(k_lo[:, TB:TB + CHUNK].bitcast(mybir.dt.uint32), 0).then_inc(drained[2], 1)
            V.memset(v_t[:, TB:TB + CHUNK], 0.0).then_inc(kvhead_ready, 1)
            V.memset(q_hi[:, :, :].bitcast(mybir.dt.uint32), 0)
            V.memset(q_lo[:, :, :].bitcast(mybir.dt.uint32), 0)
            V.memset(mask0[:, :], NEG).then_inc(uf_ready, 1)
            dve.wait_ge(consts_loaded, 16 * (CW + 4))
            V.tensor_scalar(nsink[:, :], sink[:, :], -1.0, None, ALU.mult).then_inc(consts_made, 1)
            row_scale(0)
            for s in range(2):
                split_lo(0, s, s, ahead=0)
            with dve.Fori(0, KT // 2) as i:
                norm_lo(0, i)
            dve.wait_ge(consts_made, 1)

            def body(b, last):
                with dve.Fori(0, KT) as i:
                    j = i * 4
                    n = b * KT + i
                    split_lo(b, j, 0)
                    tail = cx_tail[:, bass.ds(i, 1), :].squeeze(1)
                    V.tensor_copy(cx[:, 0:CW - 1], tail)
                    dve.wait_ge(drained[0], b * NU01 + i + 2)
                    dve.wait_ge(job_done, b * NJ + j + 2)
                    V.tensor_tensor(cx[:, CW - 1:], bank[1][:, :], xa_s, ALU.mult).then_inc(drained[1], 1)
                    split_lo(b, j + 1, 1)
                    dve.wait_ge(drained[1], b * NU01 + i + 2)
                    V.tensor_scalar(t_a, cx[:, 2:2 + TB], taps[:, 2, bass.ds(i, 1)], None, ALU.mult).then_inc(tap2_done, 1)
                    V.tensor_copy(tail, cx[:, TB:])
                    dve.wait_ge(tap2_done, n + 1)
                    V.scalar_tensor_tensor(t_b, cx[:, 1:1 + TB], taps[:, 1, bass.ds(i, 1)], t_a,
                                           ALU.mult, ALU.add).then_inc(tap1_done, 1)
                    dve.wait_ge(tap1_done, n + 1)
                    V.scalar_tensor_tensor(t_a, cx[:, 0:TB], taps[:, 0, bass.ds(i, 1)], t_b,
                                           ALU.mult, ALU.add).then_inc(tap0_done, 1)
                    split_lo(b, j + 2, 0)
                    dve.wait_ge(tanh_ready, b * (KT + NPAIR) + i + 1)
                    V.scalar_tensor_tensor(sg, th, 1.0, bank[2][:, :], ALU.add, ALU.mult).then_inc(drained[2], 1)
                    dve.wait_ge(drained[2], n + 2)
                    dve.wait_ge(tap0_done, n + 1)
                    V.tensor_tensor(v_s, sg, t_a, ALU.mult).then_inc(gate_ready, 1)
                    dve.wait_ge(job_done, b * NJ + j + 4)
                    dve.wait_ge(gate_ready, n + 1)
                    V.tensor_tensor(u_f, bank[3][:, :], v_s, ALU.mult).then_inc(uf_ready, 1)
                    split_lo(b, j + 3, 1)
                    dve.wait_ge(uhi_ready, b * 2 * KT + i + 1)
                    V.scalar_tensor_tensor(at(u_lo, i), u_f, 0.5, f(at(u_hi, i)), ALU.mult,
                                           ALU.subtract).then_inc(ulo_ready, 1)
                with dve.Fori(0, KT) as i:
                    j = i * 2 + J_CA
                    split_lo(b, j, 0)
                    dve.wait_ge(drained[0], b * NU01 + i + U_CA + 2)
                    dve.wait_ge(job_done, b * NJ + j + 2)
                    V.scalar_tensor_tensor(at(m_a, i), th, 1.0, bank[1][:, :], ALU.add, ALU.mult).then_inc(drained[1], 1)
                    split_lo(b, j + 1, 1)
                V.tensor_copy(k_lo[:, 0:CHUNK], f(k_lo[:, TB:TB + CHUNK])).then_inc(klo_tail_moved, 1)
                dve.wait_ge(khi_ready, b + 1)
                dve.wait_ge(klo_tail_moved, b + 1)
                V.tensor_tensor(k_lo[:, CHUNK:], bank[0][:, :], f(k_hi[:, CHUNK:]), ALU.subtract).then_inc(drained[0], 1)
                split_lo(b, J_KV, 0)
                split_lo(b, J_KV + 1, 1)

                def q_low(j):
                    dve.wait_ge(qhi_ready, b * NPAIR + j + 1)
                    q = bank[0][:, :].rearrange("p (c n) -> p c n", n=CHUNK)
                    for g in range(2):
                        r = slice(g * HD, (g + 1) * HD)
                        d = (r, slice(None), slice(g * CHUNK, (g + 1) * CHUNK))
                        i_ = V.tensor_tensor(q_lo[d], q[r], f(q_hi[d]), ALU.subtract)
                    i_.then_inc(drained[0], 1)

                def maxima(j, ncol):
                    n = (b * NPAIR + j) * NU
                    dve.wait_ge(scores_done, n + 1)
                    V.tensor_scalar(aux[:, 0, 0:CHUNK], aux[:, 0, 0:CHUNK], mask0[:, :], None, ALU.add).then_inc(masked, 1)
                    dve.wait_ge(masked, b * NPAIR + j + 1)
                    for u in range(NU):
                        dve.wait_ge(scores_done, n + u + 1)
                        V.tensor_reduce(mx[:, u, :], aux[:, u, :].rearrange("p (c n) -> p c n", n=P),
                                        AX.X, ALU.max).then_inc(max_ready, 1)
                    for u in range(NU):
                        dve.wait_ge(max_ready, n + u + 1)
                        V.tensor_scalar(negm[:, u, :], mx[:, u, :], -SCALE, ncol, ALU.mult, ALU.min).then_inc(negm_ready, 1)

                def normalise(j):
                    n = (b * NPAIR + j) * NU
                    for u in range(NU):
                        dve.wait_ge(exp_done, n + u + 1)
                        V.tensor_tensor(den[:, u, :], esum[:, u, :], esink[:, u, :], ALU.add).then_inc(den_ready, 1)
                        dve.wait_ge(den_ready, n + u + 1)
                        V.reciprocal(rden[:, u, :], den[:, u, :]).then_inc(rden_ready, 1)
                        dve.wait_ge(rden_ready, n + u + 1)
                        pr = p_s[u].rearrange("p (c n) -> p c n", n=P)
                        V.tensor_tensor(pr, pr, rden[:, u, :].unsqueeze(2).to_broadcast([P, UNIT, P]),
                                        ALU.mult).then_inc(probs_ready, 1)

                def gate(j):
                    dve.wait_ge(uf_ready, b * 2 * KT + KT + j + 1)
                    dve.wait_ge(tanh_ready, b * (KT + NPAIR) + KT + j + 1)
                    V.scalar_tensor_tensor(sg, th, 1.0, bank[1][:, :], ALU.add, ALU.mult).then_inc(drained[1], 1)

                def probs_lo(j):
                    for u in range(NU):
                        dve.wait_ge(pthi_ready, (b * NPAIR + j) * NU + u + 1)
                        V.tensor_tensor(pt_lo[:, u, :], aux[:, 2 + u, :], f(pt_hi[:, u, :]), ALU.subtract).then_inc(ptlo_ready, 1)

                def attended(j):
                    dve.wait_ge(pv_done, b * NPAIR + j + 1)
                    for g in range(2):
                        r = slice(g * HD, (g + 1) * HD)
                        i_ = V.tensor_tensor(
                            u_f[r].rearrange("p (c n) -> p c n", n=CHUNK),
                            bank23[r].rearrange("p u (c n) -> p (u c) n", n=P)[:, :, g * CHUNK:(g + 1) * CHUNK],
                            sg[r].rearrange("p (c n) -> p c n", n=CHUNK), ALU.mult)
                    i_.then_inc(uf_ready, 1)

                split_lo(b, J_AT, 0)
                q_low(0)
                for u in range(NU):
                    dve.wait_ge(vhi_ready, b * NU + u + 1)
                    vs = slice(u * UNIT, (u + 1) * UNIT)
                    V.tensor_tensor(v_lo[:, vs, :].rearrange("p c n -> p (c n)"), aux[:, u, :],
                                    f(v_hi[:, vs, :]).rearrange("p c n -> p (c n)"), ALU.subtract).then_inc(vlo_ready, 1)
                split_lo(b, J_AT + 1, 1)
                gate(0)
                maxima(0, nsink[:, 0:1])
                normalise(0)
                with dve.Fori(1, NPAIR) as j:
                    split_lo(b, j * 2 + J_AT, 0)
                    q_low(j)
                    probs_lo(j - 1)
                    split_lo(b, j * 2 + J_AT + 1, 1)
                    maxima(j, nsink[:, bass.ds(j, 1)])
                    dve.wait_ge(drained[1], b * NU01 + j + U_AT + 1)
                    attended(j - 1)
                    gate(j)
                    u_low(b, j + (KT - 1), j - 1)
                    normalise(j)
                V.memset(mask0[:, :], 0.0)
                split_lo(b, J_CB, 0)
                probs_lo(NPAIR - 1)
                dve.wait_ge(drained[1], b * NU01 + U_CB + 1)
                attended(NPAIR - 1)
                u_low(b, KT + NPAIR - 1, NPAIR - 1)

                def merge(i):
                    n = b * KT + i
                    dve.wait_ge(job_done, b * NJ + i * 2 + J_CB + 2)
                    dve.wait_ge(drained[0], b * NU01 + i + U_CB + 2)
                    V.scalar_tensor_tensor(v_s, th, 1.0, bank[1][:, :], ALU.add, ALU.mult).then_inc(drained[1], 1)
                    dve.wait_ge(drained[1], b * NU01 + i + U_CB + 2)
                    V.tensor_tensor(u_f, v_s, at(m_a, i), ALU.add).then_inc(msum_ready, 1)
                    split_lo(b, i * 2 + J_CB + 1, 1)
                    dve.wait_ge(mhi_ready, n + 1)
                    V.scalar_tensor_tensor(at(m_lo, i), u_f, 0.5, f(at(m_hi, i)), ALU.mult, ALU.subtract).then_inc(mlo_ready, 1)

                merge(0)
                with dve.Fori(1, KT) as i:
                    split_lo(b, i * 2 + J_CB, 0)
                    merge(i)
                if not last:
                    row_scale(b + 1)

                def final(i, split=True):
                    j = i * 2 + J_FIN
                    if split:
                        split_lo(b, j, 0)
                    dve.wait_ge(job_done, b * NJ + j + 2)
                    V.tensor_copy(at(work, i, 2, 1), bank[1][:, :]).then_inc(drained[1], 1)
                    if split:
                        split_lo(b, j + 1, 1)
                    if not last:
                        norm_lo(b + 1, i)

                if last:
                    with dve.Fori(0, KT // 2 - 1) as i:
                        final(i)
                    final(KT // 2 - 1, split=False)
                else:
                    with dve.Fori(0, KT // 2) as i:
                        final(i)
                for t in range(NT):
                    a = 2 * (t % 2)
                    y = aux[:, a:a + 2, :].rearrange("p a n -> p (a n)")
                    dve.wait_ge(ors_ready, b * NT + t + 1)
                    V.scalar_tensor_tensor(y, y, rso[:, t:t + 1], gpost[:, :], ALU.mult, ALU.mult).then_inc(y_ready, 1)
                    dve.wait_ge(y_ready, b * NT + t + 1)
                    dve.wait_ge(res_loaded[t], b * 16 + 16)
                    V.tensor_tensor(xt[:, t, :], y, xt[:, t, :], ALU.add).then_inc(res_added, 1)

            blocks(dve, body)

        @block.gpsimd
        def _(pool):
            G = nc.gpsimd
            G.memset(ident[:, :], 0.0).then_inc(pool_set, 1)
            G.memset(mhalf[:, :], -0.5).then_inc(pool_set, 1)
            G.memset(inv_d[:, :], 1.0 / D).then_inc(pool_set, 1)
            G.memset(eps[:, :], EPS).then_inc(pool_set, 1)
            pool.wait_ge(pool_set, 4)
            G.affine_select(out=ident[:, :], in_=ident[:, :], compare_op=ALU.not_equal, fill=1.0, base=0,
                            pattern=[[-1, P]], channel_multiplier=1).then_inc(ident_ready, 1)

            def rstd(ss, ms, rs, want, sums, done, ready):
                pool.wait_ge(sums, want)
                G.tensor_tensor(ms, ss, inv_d[:, 0:ss.shape[1]], ALU.mult).then_inc(ready[0], 1)
                pool.wait_ge(ready[0], done * 2 + 1)
                G.tensor_tensor(ms, ms, eps[:, 0:ss.shape[1]], ALU.add).then_inc(ready[0], 1)
                pool.wait_ge(ready[0], done * 2 + 2)
                G.tensor_tensor(rs, ms, mhalf[:, 0:ss.shape[1]], ALU.pow).then_inc(ready[1], 1)

            def row_rstd(b):
                rstd(ssx[:, :], msx[:, :], rsx[:, :], b * NT + NT, xsq_done, b, (xms_done, xrs_ready))

            row_rstd(0)

            def body(b, last):
                if not last:
                    row_rstd(b + 1)
                for t in range(NT):
                    c = slice(t, t + 1)
                    rstd(sso[:, c], mso[:, c], rso[:, c], b * NT + t + 1, osq_done, b * NT + t, (oms_done, ors_ready))

            blocks(pool, body)


INPUTS = ["x", "norm_pre", "w_in", "conv_w", "sinks", "w_proj_a", "w_proj_b", "w_out", "norm_post"]


def kernel(**inputs):
    import numpy as np
    import concourse.bacc as bacc
    from concourse.bass_utils import run_bass_kernel_spmd

    nc = bacc.Bacc("TRN2", target_bir_lowering=False, num_devices=1)
    arrays, args = {}, []
    for name in INPUTS:
        a = np.ascontiguousarray(inputs[name])
        arrays[f"{name}_dram"] = a
        args.append(nc.dram_tensor(f"{name}_dram", a.shape, mybir.dt.float32, kind="ExternalInput").ap())
    shape = arrays["x_dram"].shape
    out = nc.dram_tensor("out_dram", shape, mybir.dt.float32, kind="ExternalOutput").ap()
    hybrid_trunk(nc, *args, out)
    r = run_bass_kernel_spmd(nc, [arrays], core_ids=[0])
    return r.results[0]["out_dram"]
```

```python
import concourse.bass as bass
from concourse import mybir
from contextlib import ExitStack


def hybrid_trunk(nc, x, norm_pre, w_in, conv_w, sinks, w_proj_a, w_proj_b, w_out, norm_post, out):
    f32, f32r = mybir.dt.float32, mybir.dt.float32r
    ACT, ALU, AX = mybir.ActivationFunctionType, mybir.AluOpType, mybir.AxisListType

    P = 128
    _, S, D = x.shape
    KT = D // P
    TB = 512
    NB = S // TB
    NT = TB // P
    CHUNK, HD = 64, 64
    NC = TB // CHUNK
    UNIT = 4
    NU = NC // UNIT
    NH = sinks.shape[1]
    NPAIR = NH // 2
    CW = conv_w.shape[1]
    DKV = (w_in.shape[2] - 8 * D) // 2
    SCALE = HD ** -0.5
    WARM = 22
    EPS = 1e-6
    NEG = -1e30
    assert DKV == P and CW == 3 and NPAIR * HD * 2 == D

    C_XA, C_B, C_C, C_ZA, C_Q = 0, D, 2 * D, 3 * D, 4 * D
    C_K = 5 * D
    C_V = C_K + DKV
    C_ZB = C_V + DKV
    C_GA = C_ZB + D
    C_GB = C_GA + D

    J_CONV = 0
    J_CA = J_CONV + 4 * KT
    J_KV = J_CA + 2 * KT
    J_AT = J_KV + 2
    J_CB = J_AT + 2 * NPAIR
    J_FIN = J_CB + 2 * KT
    NJ = J_FIN + KT
    U_CONV, U_CA, U_KV = 0, KT, 2 * KT
    U_AT = U_KV + 1
    U_CB = U_AT + NPAIR
    U_FIN = U_CB + KT
    NU01 = U_FIN + KT // 2

    win = w_in[0].rearrange("(t p) n -> p t n", p=P)
    wpa = w_proj_a[0].rearrange("(t p) n -> p t n", p=P)
    wpb = w_proj_b[0].rearrange("(g j d) n -> g d j n", g=2, d=HD)
    wo = w_out[0].rearrange("(t p) n -> p t n", p=P)
    x_tiles = x.rearrange("a (t p) d -> (a t) p d", p=P)
    out_tiles = out.rearrange("a (t p) d -> (a t) p d", p=P)

    with ExitStack() as ctx:
        def sb(name, shape, dt=f32):
            return ctx.enter_context(nc.sbuf_tensor(name, shape, dt))

        def sem(name):
            return ctx.enter_context(nc.semaphore(name))

        h_hi, h_lo = sb("h_hi", [P, KT, TB], f32r), sb("h_lo", [P, KT, TB], f32r)
        u_hi, u_lo = sb("u_hi", [P, KT, TB], f32r), sb("u_lo", [P, KT, TB], f32r)
        m_hi, m_lo = sb("m_hi", [P, KT, TB], f32r), sb("m_lo", [P, KT, TB], f32r)
        pt_hi = m_hi[:, 0:2 * NU, :].rearrange("p (j u) n -> p j u n", u=NU)
        pt_lo = m_lo[:, 0:2 * NU, :].rearrange("p (j u) n -> p j u n", u=NU)
        m_a = sb("m_a", [P, KT, TB])
        xn = m_a[:, :, :].rearrange("p k n -> p (k n)").rearrange("p (t d) -> p t d", t=NT)
        xa_s, th_c, sg_c, v_s, t_a, t_b, uf_c = (m_a[:, n, :] for n in range(7))
        w_raw = sb("w_raw", [P, 2, KT, P])
        w_hi, w_lo = sb("w_hi", [P, 2, KT, P], f32r), sb("w_lo", [P, 2, KT, P], f32r)
        work = sb("work", [P, KT, TB])
        y = work[:, :, :].rearrange("p k n -> p (k n)").rearrange("p (t d) -> p t d", t=NT)
        th, sg, u_f, p_s = ([work[:, 2 * n + k, :] for k in range(2)] for n in range(4))
        o_s = sb("o_s", [P, 2, TB])
        cx = sb("cx", [P, CW - 1 + TB])
        cx_tail = sb("cx_tail", [P, KT, CW - 1])
        keys = sb("keys", [P, 2, CHUNK + TB], f32r)
        v_t = sb("v_t", [P, CHUNK + TB])
        v_hi, v_lo = sb("v_hi", [P, NC, P], f32r), sb("v_lo", [P, NC, P], f32r)
        q_hi, q_lo = sb("q_hi", [P, NC, P], f32r), sb("q_lo", [P, NC, P], f32r)
        xt = sb("xt", [P, 4, D])
        ident = sb("ident", [P, P])
        gpost = sb("gpost", [P, D])
        gpre = sb("gpre", [P, KT])
        taps = sb("taps", [P, CW, KT])
        sink = sb("sink", [P, NPAIR])
        nsink = sb("nsink", [P, NPAIR])
        mask0 = sb("mask0", [P, 1])
        mx = sb("mx", [P, NU, UNIT])
        negm = sb("negm", [P, NU, UNIT])
        esum = sb("esum", [P, NU, UNIT])
        esink = sb("esink", [P, NU, UNIT])
        den = sb("den", [P, NU, UNIT])
        rden = sb("rden", [P, NU, UNIT])
        ssx = sb("ssx", [P, NT])
        msx = sb("msx", [P, NT])
        rsx = sb("rsx", [P, NT])
        sso, sso_end = sb("sso", [P, NT]), sb("sso_end", [P, NT])
        mso = sb("mso", [P, NT])
        rso = sb("rso", [P, NT])
        mhalf, inv_d, eps = sb("mhalf", [P, NT]), sb("inv_d", [P, NT]), sb("eps", [P, NT])

        bank = ctx.enter_context(nc.psum_tensor("bank", [P, 8, TB], f32))
        VAL, TR, SC = 2, 4, 6

        raw_loaded = [sem(f"raw_loaded{n}") for n in range(2)]
        whi_ready, wlo_ready = sem("whi_ready"), sem("wlo_ready")
        job_done = sem("job_done")
        drained = [sem(f"drained{n}") for n in range(3)]
        consts_loaded, consts_made = sem("consts_loaded"), sem("consts_made")
        pool_set, ident_ready = sem("pool_set"), sem("ident_ready")
        x_loaded = [sem(f"x_loaded{n}") for n in range(NT)]
        res_loaded = [sem(f"res_loaded{n}") for n in range(NT)]
        stored = [sem(f"stored{n}") for n in range(NT)]
        xsq_done, xms_done, xrs_ready, xn_ready = map(sem, ("xsq_done", "xms_done", "xrs_ready", "xn_ready"))
        xT_done, hhi_ready, hlo_ready = map(sem, ("xT_done", "hhi_ready", "hlo_ready"))
        tap2_done, tap1_done, tap0_done = map(sem, ("tap2_done", "tap1_done", "tap0_done"))
        tanh_ready, gate_ready, bgate_ready = map(sem, ("tanh_ready", "gate_ready", "bgate_ready"))
        uf_ready, uhi_ready, ulo_ready = map(sem, ("uf_ready", "uhi_ready", "ulo_ready"))
        kvhead_ready, khi_ready, vT_done, vhi_ready, vlo_ready = map(
            sem, ("kvhead_ready", "khi_ready", "vT_done", "vhi_ready", "vlo_ready"))
        tails_moved = sem("tails_moved")
        qhi_ready = sem("qhi_ready")
        scores_done, masked, max_ready, negm_ready, exp_done = map(
            sem, ("scores_done", "masked", "max_ready", "negm_ready", "exp_done"))
        den_ready, rden_ready, probs_ready = map(sem, ("den_ready", "rden_ready", "probs_ready"))
        pT_done, pthi_ready, ptlo_ready, pv_done = map(sem, ("pT_done", "pthi_ready", "ptlo_ready", "pv_done"))
        mf_ready, msum_ready, mhi_ready, mlo_ready = map(sem, ("mf_ready", "msum_ready", "mhi_ready", "mlo_ready"))
        oT_done, osq_done, oms_done, ors_ready, y_ready, res_added = map(
            sem, ("oT_done", "osq_done", "oms_done", "ors_ready", "y_ready", "res_added"))
        last_scaled = sem("last_scaled")
        rows_ready = [sem(f"rows_ready{n}") for n in range(2)]

        def columns(at, n):
            return slice(at, at + n) if isinstance(at, int) else bass.ds(at, n)

        def column(tensor, k):
            return tensor[:, columns(k, 1)]

        def column2(tensor, n, k):
            return tensor[:, n, columns(k, 1)]

        def tile(tensor, k):
            return tensor[:, k, :] if isinstance(k, int) else tensor[:, bass.ds(k, 1), :].squeeze(1)

        def f(ap):
            return ap.bitcast(f32)

        def blocks(eng, body):
            with eng.Fori(0, NB - 1) as b:
                body(b, False)
            body(NB - 1, True)

        block = ctx.enter_context(nc.Block())

        @block.sync
        def _(sp):
            def load(slot, parts):
                for dst, src in parts:
                    sp.dma_start(dst, src).then_inc(raw_loaded[slot], 16)

            def cols(slot, src, at):
                h = KT // 2
                return [(w_raw[:, slot, k * h:(k + 1) * h, :], src[:, k * h:(k + 1) * h, bass.ds(at, P)])
                        for k in (1, 0)]

            def head_cols(slot, base, j):
                return [(w_raw[:, slot, :, g * HD:(g + 1) * HD],
                         win[:, :, bass.ds(j * HD + base + g * NPAIR * HD, HD)]) for g in range(2)]

            def head_rows(slot, at):
                return [(w_raw[g * HD:(g + 1) * HD, slot, :, :], wpb[g][:, :, bass.ds(at, P)])
                        for g in (1, 0)]

            def rows(tiles, b, t):
                return tiles[b * NT + t] if isinstance(b, int) else tiles[bass.ds(b * NT + t, 1)].squeeze(0)

            def column(at):
                return at if isinstance(at, int) else sp.snap(at)

            def slot_free(b, j):
                sp.wait_ge(wlo_ready, b * NJ + j - 1)

            def x_rows(b):
                for t in range(NT):
                    sp.dma_start(xt[:, t, :], rows(x_tiles, b, t)).then_inc(x_loaded[t], 16)

            def residual(b, t):
                sp.dma_start(xt[:, t, :], rows(x_tiles, b, t)).then_inc(res_loaded[t], 16)

            def conv(b, i, s0, s1, first=False):
                for s in range(s0, s1):
                    at = column(i * P + (C_XA, C_C, C_ZA, C_B)[s])
                    if not first:
                        slot_free(b, i * 4 + s)
                    load(s % 2, cols(s % 2, win, at))

            x_rows(0)
            conv(0, 0, 0, 1, first=True)
            with nc.allow_non_contiguous_dma(reason="small constants, once"):
                sp.dma_start(gpre[:, :], norm_pre[0].rearrange("(t p) -> p t", p=P)).then_inc(consts_loaded, 16)
                for w in range(CW):
                    sp.dma_start(taps[:, w, :], conv_w[0, w].rearrange("(t p) -> p t", p=P)).then_inc(consts_loaded, 16)
                for a in range(2):
                    for g in range(2):
                        sp.dma_start(sink[a * HD:(a + 1) * HD, :].rearrange("p (i g) -> p i g", g=2)[:, :, g],
                                     sinks.rearrange("o (g i a) -> g a o i", g=2, a=2)[g, a].to_broadcast(
                                         [HD, NPAIR // 2])).then_inc(consts_loaded, 16)
            sp.dma_start(gpost[:, :], norm_post[0:1, :].to_broadcast([P, D])).then_inc(consts_loaded, 16)
            conv(0, 0, 1, 2, first=True)
            conv(0, 0, 2, 4)
            with sp.Fori(1, KT) as i:
                conv(0, i, 0, 4)

            def body(b, last):
                with sp.Fori(0, KT) as i:
                    for s, (src, c) in enumerate(((win, C_GA), (wpa, 0))):
                        at = column(i * P + c)
                        slot_free(b, i * 2 + J_CA + s)
                        load(s, cols(s, src, at))
                for s, c in enumerate((C_K, C_V)):
                    slot_free(b, J_KV + s)
                    load(s, cols(s, win, c))
                with sp.Fori(0, NPAIR // 2) as i:
                    for g in range(2):
                        at = column(i * 2 * HD + (C_Q + g * NPAIR * HD))
                        slot_free(b, i * 4 + J_AT + 2 * g)
                        load(0, cols(0, win, at))
                        slot_free(b, i * 4 + J_AT + 2 * g + 1)
                        load(1, head_cols(1, C_ZB + g * HD, i * 2))
                if not last:
                    x_rows(b + 1)
                with sp.Fori(0, KT // 2) as i:
                    at = [column(i * 2 * P + s * P + C_GB) for s in range(2)]
                    at_b = [column(i * 2 * P + s * P) for s in range(2)]
                    for s in range(2):
                        slot_free(b, i * 4 + J_CB + s)
                        load(s, cols(s, win, at[s]))
                    for s in range(2):
                        slot_free(b, i * 4 + J_CB + 2 + s)
                        load(s, head_rows(s, at_b[s]))
                with sp.Fori(0, KT // 2) as i:
                    for s in range(2):
                        at = column(i * 2 * P + s * P)
                        slot_free(b, i * 2 + J_FIN + s)
                        load(s, cols(s, wo, at))
                for t in range(NT):
                    if not last:
                        sp.wait_ge(xn_ready, b * NT + NT + t + 1)
                    residual(b, t)
                if not last:
                    conv(b + 1, 0, 0, 4)
                    with sp.Fori(1, KT - 1) as i:
                        conv(b + 1, i, 0, 4)
                for t in range(NT):
                    sp.wait_ge(res_added, b * NT + t + 2)
                    sp.dma_start(rows(out_tiles, b, t), xt[:, t, :]).then_inc(stored[t], 16)
                if last:
                    for t in range(NT):
                        sp.wait_ge(stored[t], b * 16 + 16)
                else:
                    all_stored = sp.snap(b * 16 + 16)
                    slot_free(b + 1, 4 * (KT - 1))
                    for t in range(NT):
                        sp.wait_ge(stored[t], all_stored)
                    load(0, cols(0, win, (KT - 1) * P + C_XA))
                    conv(b + 1, KT - 1, 1, 4)

            blocks(sp, body)

        @block.tensor
        def _(pe):
            def job(b, j, slot, bk, use, hi, lo, ready=None, beside=None):
                pe.wait_ge(wlo_ready, b * NJ + j + 1)
                if bk < 2:
                    pe.wait_ge(drained[bk], b * NU01 + use + 1)
                elif bk == 2:
                    pe.wait_ge(drained[2], b * KT + use + 1)
                else:
                    pe.wait_ge(uf_ready, b * 2 * KT + use + 1)
                for k in range(KT):
                    if ready:
                        ready(k)
                    if k == 3 and beside:
                        beside()
                    for n, (w, a) in enumerate(((w_hi, hi), (w_hi, lo), (w_lo, hi))):
                        mm = nc.tensor.matmul(bank[:, bk, :], w[:, slot, k, :], a[:, k, :],
                                              start=(k == 0 and n == 0), stop=(k == KT - 1 and n == 2))
                mm.then_inc(job_done, 1)

            def norm_transposes(b, i, at=SC):
                for s in range(2):
                    for t in range(NT):
                        mm = nc.tensor.transpose(bank[:, at + s, t * P:(t + 1) * P],
                                                 xn[:, t, (i * 2 + s) * P:(i * 2 + s + 1) * P], ident[:, :])
                    mm.then_inc(xT_done, 1)

            def out_transposes(b, i, s):
                pe.wait_ge(drained[s], b * NU01 + i + U_FIN + 2)
                if not (isinstance(i, int) and i == 0):
                    pe.wait_ge(rows_ready[s], b * (KT // 2) + i)
                for t in range(NT):
                    mm = nc.tensor.transpose(bank[:, TR + s, t * P:(t + 1) * P],
                                             o_s[:, s, t * P:(t + 1) * P], ident[:, :])
                mm.then_inc(oT_done, 1)

            def probs_transposes(b, j, after_values):
                for u in range(NU):
                    if after_values:
                        if u == 0:
                            pe.wait_ge(uf_ready, b * 2 * KT + j + KT + 1)
                    else:
                        pe.wait_ge(ptlo_ready, (b * NPAIR + j - 1) * NU + u + 1)
                    pe.wait_ge(probs_ready, (b * NPAIR + j) * NU + u + 1)
                    for c in range(UNIT):
                        mm = nc.tensor.transpose(bank[:, TR + u, c * P:(c + 1) * P],
                                                 p_s[u][:, c * P:(c + 1) * P], ident[:, :])
                    mm.then_inc(pT_done, 1)

            def scores(b, j, g):
                pe.wait_ge(drained[0], b * NU01 + j + U_AT + 2)
                for u in range(NU):
                    for c in range(UNIT):
                        n = u * UNIT + c
                        k0 = n * CHUNK
                        for m, q in enumerate((q_hi, q_lo)):
                            mm = nc.tensor.matmul(bank[:, SC + u, c * P:(c + 1) * P], q[:, n, :],
                                                  keys[:, g, k0:k0 + 2 * CHUNK], start=(m == 0), stop=(m == 1))
                    mm.then_inc(scores_done, 1)

            def values(b, i):
                pe.wait_ge(ptlo_ready, (b * NPAIR + i * 2 + 2) * NU)
                pe.wait_ge(uf_ready, b * 2 * KT + i * 2 + KT + 1)
                for n in range(NC):
                    u, c = n // UNIT, n % UNIT
                    for m, (v, pt) in enumerate(((v_hi, pt_hi), (v_hi, pt_lo), (v_lo, pt_hi))):
                        mm = nc.tensor.matmul(bank[:, VAL + n // 2, n % 2 * 2 * P:(n % 2 + 1) * 2 * P], v[:, n, :],
                                              pt[:, :, u, c * P:(c + 1) * P], start=(m == 0), stop=(m == 2))
                mm.then_inc(pv_done, 1)

            pe.wait_ge(ident_ready, 1)
            with pe.Fori(0, WARM):
                nc.tensor.transpose(bank[:, SC, 0:P], ident[:, :], ident[:, :])
            pe.wait_ge(xn_ready, NT)
            for i in range(KT // 2):
                if i >= 2:
                    pe.wait_ge(hlo_ready, 2 * i - 2)
                norm_transposes(0, i, at=TR + i % 2 * 2)

            def body(b, last):
                for s in range(4):
                    job(b, s, s % 2, s, U_CONV, h_hi, h_lo,
                        ready=(lambda k: pe.wait_ge(hlo_ready, b * KT + k + 1)) if s == 0 else None)
                with pe.Fori(1, KT) as i:
                    for s in range(4):
                        job(b, i * 4 + s, s % 2, s, i + U_CONV, h_hi, h_lo)
                with pe.Fori(0, KT) as i:
                    job(b, i * 2 + J_CA, 0, 0, i + U_CA, h_hi, h_lo)
                    pe.wait_ge(ulo_ready, b * 2 * KT + KT)
                    job(b, i * 2 + J_CA + 1, 1, 1, i + U_CA, u_hi, u_lo)
                job(b, J_KV, 0, 0, U_KV, h_hi, h_lo)
                job(b, J_KV + 1, 1, 1, U_KV, h_hi, h_lo)

                def query(j):
                    job(b, j * 2 + J_AT, 0, 0, j + U_AT, h_hi, h_lo)

                def z_gate(j, beside=None):
                    job(b, j * 2 + J_AT + 1, 1, 1, j + U_AT, h_hi, h_lo, beside=beside)

                query(0)
                pe.wait_ge(drained[1], b * NU01 + U_KV + 2)
                for u in range(NU):
                    for c in range(UNIT):
                        k0 = (u * UNIT + c) * CHUNK
                        mm = nc.tensor.transpose(bank[:, SC + u, c * P:(c + 1) * P], v_t[:, k0:k0 + 2 * CHUNK], ident[:, :])
                    mm.then_inc(vT_done, 1)
                z_gate(0)
                pe.wait_ge(vlo_ready, b * NU + NU)
                scores(b, 0, 0)
                query(1)
                z_gate(1, lambda: probs_transposes(b, 0, True))
                scores(b, 1, 1)
                with pe.Fori(1, NPAIR // 2) as i:
                    j = i * 2
                    query(j)
                    z_gate(j, lambda: probs_transposes(b, j - 1, False))
                    scores(b, j, 0)
                    values(b, i - 1)
                    query(j + 1)
                    z_gate(j + 1, lambda: probs_transposes(b, j, True))
                    scores(b, j + 1, 1)

                def merge(i, first=False, ready=None):
                    job(b, i * 4 + J_CB, 0, 0, i * 2 + U_CB, h_hi, h_lo)
                    job(b, i * 4 + J_CB + 1, 1, 1, i * 2 + U_CB, h_hi, h_lo,
                        beside=(lambda: probs_transposes(b, NPAIR - 1, False)) if first else None)
                    if first:
                        values(b, NPAIR // 2 - 1)
                    job(b, i * 4 + J_CB + 2, 0, 0, i * 2 + U_CB + 1, u_hi, u_lo, ready=ready)
                    job(b, i * 4 + J_CB + 3, 1, 1, i * 2 + U_CB + 1, u_hi, u_lo)

                merge(0, first=True, ready=lambda k: k >= KT - 2 and pe.wait_ge(ulo_ready, b * 2 * KT + KT + k + 1))
                with pe.Fori(1, KT // 2) as i:
                    merge(i)

                def final(i, ready=None):
                    job(b, i * 2 + J_FIN, 0, 0, i + U_FIN, m_hi, m_lo, ready=ready,
                        beside=None if isinstance(i, int) and i == 0 else lambda: out_transposes(b, i - 1, 1))
                    job(b, i * 2 + J_FIN + 1, 1, 1, i + U_FIN, m_hi, m_lo, beside=lambda: out_transposes(b, i, 0))
                    if not last:
                        pe.wait_ge(xn_ready, b * NT + 2 * NT)
                        if i:
                            pe.wait_ge(hlo_ready, b * KT + KT + i * 2)
                        norm_transposes(b + 1, i)

                pe.wait_ge(mlo_ready, b * KT + KT - 2)
                final(0, ready=lambda k: k >= KT - 2 and pe.wait_ge(mlo_ready, b * KT + k + 1))
                if last:
                    with pe.Fori(1, KT // 2) as i:
                        final(i)
                else:
                    for i in range(1, KT // 2):
                        final(i)
                out_transposes(b, KT // 2 - 1, 1)

            blocks(pe, body)

        @block.scalar
        def _(act):
            def split_hi(b, j, slot, ahead=2):
                n = j + ahead
                act.wait_ge(raw_loaded[slot], b * (NJ * 16) + (n - slot) * 16 + 32)
                if ahead:
                    act.wait_ge(job_done, b * NJ + j + 1)
                nc.scalar.activation(w_hi[:, slot], w_raw[:, slot], ACT.Copy).then_inc(whi_ready, 1)

            def row_squares(b, tiles):
                for t in tiles:
                    act.wait_ge(x_loaded[t], b * 16 + 16)
                    nc.scalar.activation((q_hi, q_lo, v_hi, v_lo)[t][:, :, :].rearrange("p c n -> p (c n)"),
                                         xt[:, t, :], ACT.Square, accum_out=ssx[:, t:t + 1]).then_inc(xsq_done, 1)

            def norm_hi(b, i, at=SC):
                for s in range(2):
                    act.wait_ge(xT_done, b * KT + i * 2 + s + 1)
                    nc.scalar.activation(tile(h_hi, i * 2 + s), bank[:, at + s, :], ACT.Copy,
                                         scale=column(gpre, i * 2 + s)).then_inc(hhi_ready, 1)

            def probs_hi(b, j, par):
                for u in range(NU):
                    act.wait_ge(pT_done, (b * NPAIR + j) * NU + u + 1)
                    nc.scalar.activation(pt_hi[:, par, u, :], bank[:, TR + u, :], ACT.Copy).then_inc(pthi_ready, 1)

            def u_high(b, n, k, uf):
                act.wait_ge(uf_ready, b * 2 * KT + n + 2)
                nc.scalar.activation(tile(u_hi, k), uf, ACT.Copy, scale=0.5).then_inc(uhi_ready, 1)

            def exps(b, j, jcol):
                for u in range(NU):
                    act.wait_ge(negm_ready, (b * NPAIR + j) * NU + u + 1)
                    for c in range(UNIT):
                        nc.scalar.activation(p_s[u][:, c * P:(c + 1) * P], bank[:, SC + u, c * P:(c + 1) * P], ACT.Exp,
                                             bias=negm[:, u, c:c + 1], scale=SCALE, accum_out=esum[:, u, c:c + 1])
                    nc.scalar.activation(esink[:, u, :], negm[:, u, :], ACT.Exp,
                                         bias=jcol).then_inc(exp_done, 1)

            row_squares(0, range(NT))
            split_hi(0, 0, 0, ahead=0)
            act.wait_ge(consts_loaded, 16 * (CW + 6))
            for i in range(KT // 2):
                norm_hi(0, i, at=TR + i % 2 * 2)
                if i == 1:
                    split_hi(0, 1, 1, ahead=0)

            def body(b, last):
                with act.Fori(0, KT) as i:
                    j = i * 4
                    split_hi(b, j, 0)
                    act.wait_ge(drained[1], b * NU01 + i + 1)
                    nc.scalar.activation(xa_s, bank[:, 0, :], ACT.Copy).then_inc(drained[0], 1)
                    split_hi(b, j + 1, 1)
                    split_hi(b, j + 2, 0)
                    act.wait_ge(drained[2], b * KT + i + 1)
                    nc.scalar.activation(th_c, bank[:, 2, :], ACT.Tanh, scale=0.5).then_inc(tanh_ready, 1)
                    split_hi(b, j + 3, 1)
                    u_high(b, i, i, uf_c)

                with act.Fori(0, KT) as i:
                    j = i * 2 + J_CA
                    split_hi(b, j, 0)
                    act.wait_ge(res_added, b * NT + 1)
                    act.wait_ge(drained[1], b * NU01 + i + U_CA + 1)
                    nc.scalar.activation(th[0], bank[:, 0, :], ACT.Tanh, scale=0.5).then_inc(drained[0], 1)
                    split_hi(b, j + 1, 1)
                act.wait_ge(kvhead_ready, 1)
                nc.scalar.activation(keys[:, :, 0:CHUNK], f(keys[:, :, TB:TB + CHUNK]), ACT.Copy)
                nc.scalar.activation(v_t[:, 0:CHUNK], v_t[:, TB:TB + CHUNK], ACT.Copy).then_inc(tails_moved, 1)
                split_hi(b, J_KV, 0)
                act.wait_ge(tails_moved, b + 1)
                for g in range(2):
                    r = slice(g * HD, (g + 1) * HD)
                    nc.scalar.activation(keys[r, g, CHUNK:], bank[r, 0, :], ACT.Copy).then_inc(khi_ready, 1)
                split_hi(b, J_KV + 1, 1)
                nc.scalar.activation(v_t[:, CHUNK:], bank[:, 1, :], ACT.Copy).then_inc(drained[1], 1)

                def q_high(j):
                    act.wait_ge(job_done, b * NJ + j * 2 + J_AT + 1)
                    q = bank[:, 0, :].rearrange("p (c n) -> p c n", n=CHUNK)
                    for own in (True, False):
                        for a in range(2):
                            r = slice(a * HD, (a + 1) * HD)
                            to = r if own else slice((1 - a) * HD, (2 - a) * HD)
                            nc.scalar.activation(q_hi[to, :, a * CHUNK:(a + 1) * CHUNK], q[r], ACT.Copy).then_inc(qhi_ready, 1)

                def z_tanh(j):
                    act.wait_ge(drained[1], b * NU01 + j + U_AT + 1)
                    nc.scalar.activation(th[0], bank[:, 1, :], ACT.Tanh, scale=0.5).then_inc(tanh_ready, 1)

                def u_highs(i):
                    for k in range(2):
                        u_high(b, i * 2 + (KT + k), i * 2 + k, u_f[k])

                q_high(0)
                for u in range(NU):
                    act.wait_ge(vT_done, b * NU + u + 1)
                    nc.scalar.activation(v_hi[:, u * UNIT:(u + 1) * UNIT, :].rearrange("p c n -> p (c n)"),
                                         bank[:, SC + u, :], ACT.Copy).then_inc(vhi_ready, 1)
                split_hi(b, J_AT, 0)
                split_hi(b, J_AT + 1, 1)
                z_tanh(0)
                exps(b, 0, sink[:, 0:1])

                def second(j):
                    q_high(j + 1)
                    split_hi(b, j * 2 + J_AT + 2, 0)
                    probs_hi(b, j, 0)
                    split_hi(b, j * 2 + J_AT + 3, 1)
                    z_tanh(j + 1)
                    exps(b, j + 1, column(sink, j + 1))

                second(0)
                with act.Fori(1, NPAIR // 2) as i:
                    j = i * 2
                    q_high(j)
                    split_hi(b, j * 2 + J_AT, 0)
                    probs_hi(b, j - 1, 1)
                    split_hi(b, j * 2 + J_AT + 1, 1)
                    z_tanh(j)
                    exps(b, j, column(sink, j))
                    u_highs(i - 1)
                    second(j)

                def m_high(i, k):
                    act.wait_ge(msum_ready, b * KT + i * 2 + k + 1)
                    nc.scalar.activation(tile(m_hi, i * 2 + k), u_f[k], ACT.Copy, scale=0.5).then_inc(mhi_ready, 1)

                def merge(i, first=False):
                    j = i * 4 + J_CB
                    split_hi(b, j, 0)
                    act.wait_ge(drained[1], b * NU01 + i * 2 + U_CB + 1)
                    nc.scalar.activation(th[0], bank[:, 0, :], ACT.Tanh, scale=0.5).then_inc(drained[0], 1)
                    if first:
                        probs_hi(b, NPAIR - 1, 1)
                    split_hi(b, j + 1, 1)
                    nc.scalar.activation(th[1], bank[:, 1, :], ACT.Tanh, scale=0.5).then_inc(drained[1], 1)
                    if first:
                        u_highs(NPAIR // 2 - 1)
                    split_hi(b, j + 2, 0)
                    m_high(i, 0)
                    split_hi(b, j + 3, 1)
                    m_high(i, 1)

                merge(0, first=True)
                if not last:
                    row_squares(b + 1, range(NT // 2))
                with act.Fori(1, KT // 2) as i:
                    merge(i)
                if not last:
                    row_squares(b + 1, range(NT // 2, NT))

                def final(i, split=True):
                    j = i * 2 + J_FIN
                    if split:
                        split_hi(b, j, 0)
                    act.wait_ge(job_done, b * NJ + j + 1)
                    if not (isinstance(i, int) and i == 0):
                        act.wait_ge(oT_done, b * KT + i * 2 - 1)
                    nc.scalar.activation(o_s[:, 0, :], bank[:, 0, :], ACT.Copy).then_inc(drained[0], 1)
                    act.wait_ge(oT_done, b * KT + i * 2 + 1)
                    nc.scalar.activation(y[:, :, columns(i * 2 * P, P)],
                                         bank[:, TR, :].rearrange("p (t n) -> p t n", n=P), ACT.Copy
                                         ).then_inc(rows_ready[0], 1)
                    if split:
                        split_hi(b, j + 1, 1)
                    if not last:
                        norm_hi(b + 1, i)

                def out_squares(src, t, sums):
                    to = (u_lo if last else m_lo)[:, 2 * t:2 * t + 2, :].rearrange("p a n -> p (a n)")
                    nc.scalar.activation(to[:, 0:src.shape[1]], src, ACT.Square, accum_out=sums).then_inc(osq_done, 1)

                final(0)
                with act.Fori(1, KT // 2 - 1) as i:
                    final(i)
                final(KT // 2 - 1, split=not last)
                if not last:
                    for k in range(2):
                        act.wait_ge(rows_ready[k], b * (KT // 2) + KT // 2)
                    for t in range(NT):
                        out_squares(y[:, t, :], t, sso[:, t:t + 1])
                else:
                    act.wait_ge(rows_ready[0], (b + 1) * (KT // 2))
                    act.wait_ge(rows_ready[1], (b + 1) * (KT // 2) - 1)
                    for t in range(NT):
                        out_squares(y[:, t, 0:D - P], t, sso[:, t:t + 1])
                    act.wait_ge(oT_done, (b + 1) * KT)
                    act.wait_ge(osq_done, (b + 1) * NT)
                    for t in range(NT):
                        out_squares(bank[:, TR + 1, t * P:(t + 1) * P], t, sso_end[:, t:t + 1])

            blocks(act, body)

        @block.vector
        def _(dve):
            V = nc.vector

            def split_lo(b, j, slot, ahead=2):
                n = j + ahead
                dve.wait_ge(whi_ready, b * NJ + n + 1)
                V.tensor_tensor(w_lo[:, slot], w_raw[:, slot], f(w_hi[:, slot]), ALU.subtract).then_inc(wlo_ready, 1)

            def row_scale(b):
                for t in range(NT):
                    dve.wait_ge(xrs_ready, b * NT + t + 1)
                    V.tensor_scalar(xn[:, t, :], xt[:, t, :], rsx[:, t:t + 1], None, ALU.mult).then_inc(xn_ready, 1)

            def norm_lo(b, i, at=SC):
                for s in range(2):
                    dve.wait_ge(hhi_ready, b * KT + i * 2 + s + 1)
                    k = i * 2 + s
                    V.scalar_tensor_tensor(tile(h_lo, k), bank[:, at + s, :], column(gpre, k),
                                           f(tile(h_hi, k)), ALU.mult, ALU.subtract).then_inc(hlo_ready, 1)

            def u_low(b, n, k, uf):
                dve.wait_ge(uhi_ready, b * 2 * KT + n + 1)
                V.scalar_tensor_tensor(tile(u_lo, k), uf, 0.5, f(tile(u_hi, k)), ALU.mult,
                                       ALU.subtract).then_inc(ulo_ready, 1)

            V.memset(cx_tail[:, :, :], 0.0).then_inc(drained[0], 1)
            V.memset(keys[:, :, TB:TB + CHUNK].bitcast(mybir.dt.uint32), 0).then_inc(drained[1], 1)
            V.memset(sso_end[:, :], 0.0).then_inc(drained[2], 1)
            V.memset(v_t[:, TB:TB + CHUNK], 0.0).then_inc(kvhead_ready, 1)
            V.memset(mask0[:, :], NEG).then_inc(uf_ready, 1)
            row_scale(0)
            split_lo(0, 0, 0, ahead=0)
            dve.wait_ge(consts_loaded, 16 * (CW + 6))
            for i in range(KT // 2):
                norm_lo(0, i, at=TR + i % 2 * 2)
                if i == 1:
                    split_lo(0, 1, 1, ahead=0)
            V.tensor_scalar(nsink[:, :], sink[:, :], -1.0, None, ALU.mult).then_inc(consts_made, 1)
            dve.wait_ge(consts_made, 1)

            def body(b, last):
                with dve.Fori(0, KT) as i:
                    j = i * 4
                    n = b * KT + i
                    split_lo(b, j, 0)
                    tail = tile(cx_tail, i)
                    V.tensor_copy(cx[:, 0:CW - 1], tail)
                    dve.wait_ge(drained[0], b * NU01 + i + 2)
                    dve.wait_ge(job_done, b * NJ + j + 2)
                    V.tensor_tensor(cx[:, CW - 1:], bank[:, 1, :], xa_s, ALU.mult).then_inc(drained[1], 1)
                    split_lo(b, j + 1, 1)
                    dve.wait_ge(drained[1], b * NU01 + i + 2)
                    V.tensor_scalar(t_a, cx[:, 2:2 + TB], column2(taps, 2, i), None, ALU.mult).then_inc(tap2_done, 1)
                    V.tensor_copy(tail, cx[:, TB:])
                    dve.wait_ge(tap2_done, n + 1)
                    V.scalar_tensor_tensor(t_b, cx[:, 1:1 + TB], column2(taps, 1, i), t_a,
                                           ALU.mult, ALU.add).then_inc(tap1_done, 1)
                    dve.wait_ge(tap1_done, n + 1)
                    V.scalar_tensor_tensor(t_a, cx[:, 0:TB], column2(taps, 0, i), t_b,
                                           ALU.mult, ALU.add).then_inc(tap0_done, 1)
                    split_lo(b, j + 2, 0)
                    dve.wait_ge(tanh_ready, b * (KT + NPAIR) + i + 1)
                    V.scalar_tensor_tensor(sg_c, th_c, 1.0, bank[:, 2, :], ALU.add, ALU.mult).then_inc(drained[2], 1)
                    dve.wait_ge(drained[2], n + 2)
                    dve.wait_ge(tap0_done, n + 1)
                    V.tensor_tensor(v_s, sg_c, t_a, ALU.mult).then_inc(gate_ready, 1)
                    dve.wait_ge(job_done, b * NJ + j + 4)
                    dve.wait_ge(gate_ready, n + 1)
                    V.tensor_tensor(uf_c, bank[:, 3, :], v_s, ALU.mult).then_inc(uf_ready, 1)
                    split_lo(b, j + 3, 1)
                    u_low(b, i, i, uf_c)
                with dve.Fori(0, KT) as i:
                    j = i * 2 + J_CA
                    split_lo(b, j, 0)
                    dve.wait_ge(drained[0], b * NU01 + i + U_CA + 2)
                    dve.wait_ge(job_done, b * NJ + j + 2)
                    V.scalar_tensor_tensor(tile(m_a, i), th[0], 1.0, bank[:, 1, :], ALU.add, ALU.mult).then_inc(drained[1], 1)
                    split_lo(b, j + 1, 1)
                dve.wait_ge(khi_ready, b * 2 + 2)
                for g in range(2):
                    r, other = slice(g * HD, (g + 1) * HD), slice((1 - g) * HD, (2 - g) * HD)
                    i_ = V.tensor_tensor(keys[other, g, CHUNK:], bank[r, 0, :], f(keys[r, g, CHUNK:]), ALU.subtract)
                i_.then_inc(drained[0], 1)
                split_lo(b, J_KV, 0)
                split_lo(b, J_KV + 1, 1)

                def q_low(j):
                    dve.wait_ge(qhi_ready, (b * NPAIR + j) * 4 + 4)
                    q = bank[:, 0, :].rearrange("p (c n) -> p c n", n=CHUNK)
                    for a in range(2):
                        r, n = slice(a * HD, (a + 1) * HD), slice(a * CHUNK, (a + 1) * CHUNK)
                        for half in range(2):
                            i_ = V.tensor_tensor(q_lo[half * HD:(half + 1) * HD, :, n], q[r], f(q_hi[r, :, n]), ALU.subtract)
                    i_.then_inc(drained[0], 1)

                def maxima(j):
                    n = (b * NPAIR + j) * NU
                    dve.wait_ge(scores_done, n + 1)
                    V.tensor_scalar(bank[:, SC, 0:CHUNK], bank[:, SC, 0:CHUNK], mask0[:, :], None,
                                    ALU.add).then_inc(masked, 1)
                    dve.wait_ge(masked, b * NPAIR + j + 1)
                    for u in range(NU):
                        dve.wait_ge(scores_done, n + u + 1)
                        V.tensor_reduce(mx[:, u, :], bank[:, SC + u, :].rearrange("p (c n) -> p c n", n=P),
                                        AX.X, ALU.max).then_inc(max_ready, 1)
                        dve.wait_ge(max_ready, n + u + 1)
                        V.tensor_scalar(negm[:, u, :], mx[:, u, :], -SCALE, column(nsink, j), ALU.mult,
                                        ALU.min).then_inc(negm_ready, 1)

                def normalise(j):
                    n = (b * NPAIR + j) * NU
                    for u in range(NU):
                        dve.wait_ge(exp_done, n + u + 1)
                        V.tensor_tensor(den[:, u, :], esum[:, u, :], esink[:, u, :], ALU.add).then_inc(den_ready, 1)
                        dve.wait_ge(den_ready, n + u + 1)
                        V.reciprocal(rden[:, u, :], den[:, u, :]).then_inc(rden_ready, 1)
                        dve.wait_ge(rden_ready, n + u + 1)
                        pr = p_s[u].rearrange("p (c n) -> p c n", n=P)
                        V.tensor_tensor(pr, pr, rden[:, u, :].unsqueeze(2).to_broadcast([P, UNIT, P]),
                                        ALU.mult).then_inc(probs_ready, 1)

                def gate(j, k):
                    dve.wait_ge(tanh_ready, b * (KT + NPAIR) + KT + j + 1)
                    V.scalar_tensor_tensor(sg[k], th[0], 1.0, bank[:, 1, :], ALU.add, ALU.mult).then_inc(drained[1], 1)

                def probs_lo(j, par):
                    for u in range(NU):
                        dve.wait_ge(pthi_ready, (b * NPAIR + j) * NU + u + 1)
                        V.tensor_tensor(pt_lo[:, par, u, :], bank[:, TR + u, :], f(pt_hi[:, par, u, :]),
                                        ALU.subtract).then_inc(ptlo_ready, 1)

                def attended(i):
                    dve.wait_ge(pv_done, b * (NPAIR // 2) + i + 1)
                    dve.wait_ge(ulo_ready, b * 2 * KT + i * 2 + KT)
                    dve.wait_ge(drained[1], b * NU01 + i * 2 + U_AT + 3)
                    for k in range(2):
                        for g in range(2):
                            r = slice(g * HD, (g + 1) * HD)
                            i_ = V.tensor_tensor(
                                u_f[k][r].rearrange("p (c n) -> p c n", n=CHUNK),
                                bank[r, VAL:VAL + 4, :].rearrange("p a (c j n) -> p (a c) j n", j=2, n=P)
                                [:, :, g, k * CHUNK:(k + 1) * CHUNK],
                                sg[k][r].rearrange("p (c n) -> p c n", n=CHUNK), ALU.mult)
                        i_.then_inc(uf_ready, 1)

                def u_lows(i):
                    for k in range(2):
                        u_low(b, i * 2 + (KT + k), i * 2 + k, u_f[k])

                q_low(0)
                for u in range(NU):
                    dve.wait_ge(vhi_ready, b * NU + u + 1)
                    vs = slice(u * UNIT, (u + 1) * UNIT)
                    V.tensor_tensor(v_lo[:, vs, :].rearrange("p c n -> p (c n)"), bank[:, SC + u, :],
                                    f(v_hi[:, vs, :]).rearrange("p c n -> p (c n)"), ALU.subtract).then_inc(vlo_ready, 1)
                split_lo(b, J_AT, 0)
                split_lo(b, J_AT + 1, 1)
                gate(0, 0)
                maxima(0)
                normalise(0)

                def second(j):
                    q_low(j + 1)
                    split_lo(b, j * 2 + J_AT + 2, 0)
                    probs_lo(j, 0)
                    split_lo(b, j * 2 + J_AT + 3, 1)
                    gate(j + 1, 1)
                    maxima(j + 1)
                    normalise(j + 1)

                second(0)
                with dve.Fori(1, NPAIR // 2) as i:
                    j = i * 2
                    q_low(j)
                    split_lo(b, j * 2 + J_AT, 0)
                    probs_lo(j - 1, 1)
                    split_lo(b, j * 2 + J_AT + 1, 1)
                    maxima(j)
                    attended(i - 1)
                    dve.wait_ge(uf_ready, b * 2 * KT + KT + j + 1)
                    gate(j, 0)
                    normalise(j)
                    u_lows(i - 1)
                    second(j)
                V.memset(mask0[:, :], 0.0)

                def merge_tile(i, k):
                    n = b * KT + i * 2 + k
                    dve.wait_ge(job_done, b * NJ + i * 4 + (J_CB + 3 + k))
                    dve.wait_ge(drained[k], b * NU01 + i * 2 + U_CB + 2)
                    V.scalar_tensor_tensor(sg[k], th[k], 1.0, bank[:, k, :], ALU.add, ALU.mult).then_inc(drained[k], 1)
                    dve.wait_ge(drained[k], b * NU01 + i * 2 + U_CB + 3)
                    V.tensor_tensor(u_f[k], sg[k], tile(m_a, i * 2 + k), ALU.add).then_inc(msum_ready, 1)

                def m_low(i, k):
                    dve.wait_ge(mhi_ready, b * KT + i * 2 + k + 1)
                    V.scalar_tensor_tensor(tile(m_lo, i * 2 + k), u_f[k], 0.5, f(tile(m_hi, i * 2 + k)), ALU.mult,
                                           ALU.subtract).then_inc(mlo_ready, 1)

                def merge(i, first=False):
                    j = i * 4 + J_CB
                    split_lo(b, j, 0)
                    if first:
                        probs_lo(NPAIR - 1, 1)
                    split_lo(b, j + 1, 1)
                    if first:
                        attended(NPAIR // 2 - 1)
                        u_lows(NPAIR // 2 - 1)
                    merge_tile(i, 0)
                    split_lo(b, j + 2, 0)
                    m_low(i, 0)
                    merge_tile(i, 1)
                    m_low(i, 1)
                    split_lo(b, j + 3, 1)

                merge(0, first=True)
                with dve.Fori(1, KT // 2) as i:
                    merge(i)
                if not last:
                    row_scale(b + 1)

                def odd_rows(i):
                    dve.wait_ge(oT_done, b * KT + i * 2 + 2)
                    V.tensor_scalar(y[:, :, columns(i * 2 * P + P, P)], bank[:, TR + 1, :].rearrange("p (t n) -> p t n", n=P),
                                    1.0, None, ALU.mult).then_inc(rows_ready[1], 1)

                def final(i, split=True):
                    j = i * 2 + J_FIN
                    if not (isinstance(i, int) and i == 0):
                        odd_rows(i - 1)
                    if split:
                        split_lo(b, j, 0)
                    elif last:
                        for c, even in ((slice(0, D - 2 * P), i), (slice(D - 2 * P, D - P), i + 1)):
                            dve.wait_ge(rows_ready[0], b * (KT // 2) + even)
                            dve.wait_ge(rows_ready[1], b * (KT // 2) + i)
                            V.tensor_tensor(xn[:, :, c], y[:, :, c],
                                            gpost[:, c].unsqueeze(1).to_broadcast([P, NT, c.stop - c.start]), ALU.mult)
                    dve.wait_ge(job_done, b * NJ + j + 2)
                    if not (isinstance(i, int) and i == 0):
                        dve.wait_ge(oT_done, b * KT + i * 2)
                    V.tensor_copy(o_s[:, 1, :], bank[:, 1, :]).then_inc(drained[1], 1)
                    if split:
                        split_lo(b, j + 1, 1)
                    if not last:
                        norm_lo(b + 1, i)

                final(0)
                with dve.Fori(1, KT // 2 - 1) as i:
                    final(i)
                final(KT // 2 - 1, split=not last)
                if not last:
                    odd_rows(KT // 2 - 1)
                else:
                    dve.wait_ge(osq_done, NB * NT + NT)
                    V.tensor_tensor(mso[:, :], sso[:, :], sso_end[:, :], ALU.add).then_inc(oms_done, 1)
                    dve.wait_ge(oms_done, NT * 2 * (NB - 1) + 1)
                    V.tensor_scalar(mso[:, :], mso[:, :], 1.0 / D, EPS, ALU.mult, ALU.add).then_inc(oms_done, 1)
                    V.tensor_tensor(xn[:, :, D - P:], bank[:, TR + 1, :].rearrange("p (t n) -> p t n", n=P),
                                    gpost[:, D - P:].unsqueeze(1).to_broadcast([P, NT, P]), ALU.mult).then_inc(last_scaled, 1)
                    dve.wait_ge(last_scaled, 1)
                    for t in range(NT):
                        dve.wait_ge(ors_ready, b * NT + t + 1)
                        dve.wait_ge(res_loaded[t], b * 16 + 16)
                        V.scalar_tensor_tensor(xt[:, t, :], xn[:, t, :], rso[:, t:t + 1], xt[:, t, :], ALU.mult,
                                               ALU.add).then_inc(res_added, 1)

            blocks(dve, body)

        @block.gpsimd
        def _(pool):
            G = nc.gpsimd
            G.memset(ident[:, :], 0.0).then_inc(pool_set, 1)
            G.memset(mhalf[:, :], -0.5).then_inc(pool_set, 1)
            G.memset(inv_d[:, :], 1.0 / D).then_inc(pool_set, 1)
            G.memset(eps[:, :], EPS).then_inc(pool_set, 1)
            G.memset(mso[:, :], 0.0).then_inc(res_added, 1)
            pool.wait_ge(pool_set, 4)
            G.affine_select(out=ident[:, :], in_=ident[:, :], compare_op=ALU.not_equal, fill=1.0, base=0,
                            pattern=[[-1, P]], channel_multiplier=1).then_inc(ident_ready, 1)

            def rstd(ss, ms, rs, want, sums, done, ready):
                pool.wait_ge(sums, want)
                G.tensor_tensor(ms, ss, inv_d[:, 0:ss.shape[1]], ALU.mult).then_inc(ready[0], 1)
                pool.wait_ge(ready[0], done * 2 + 1)
                G.tensor_tensor(ms, ms, eps[:, 0:ss.shape[1]], ALU.add).then_inc(ready[0], 1)
                pool.wait_ge(ready[0], done * 2 + 2)
                G.tensor_tensor(rs, ms, mhalf[:, 0:ss.shape[1]], ALU.pow).then_inc(ready[1], 1)

            def row_rstd(b):
                for t in range(NT):
                    c = slice(t, t + 1)
                    rstd(ssx[:, c], msx[:, c], rsx[:, c], b * NT + t + 1, xsq_done, b * NT + t, (xms_done, xrs_ready))

            row_rstd(0)

            def body(b, last):
                if not last:
                    row_rstd(b + 1)
                for t in range(NT):
                    c = slice(t, t + 1)
                    if last:
                        pool.wait_ge(oms_done, NT * 2 * (NB - 1) + 2)
                        G.tensor_tensor(rso[:, c], mso[:, c], mhalf[:, c], ALU.pow).then_inc(ors_ready, 1)
                        continue
                    rstd(sso[:, c], mso[:, c], rso[:, c], b * NT + t + 1, osq_done, b * NT + t, (oms_done, ors_ready))
                    n = (b * NT + t) * 2
                    G.tensor_tensor(y[:, t, :], y[:, t, :], gpost[:, :], ALU.mult).then_inc(y_ready, 1)
                    pool.wait_ge(ors_ready, b * NT + t + 1)
                    pool.wait_ge(y_ready, n + 1)
                    G.tensor_tensor(y[:, t, :], y[:, t, :], rso[:, c].to_broadcast([P, D]), ALU.mult).then_inc(y_ready, 1)
                    pool.wait_ge(y_ready, n + 2)
                    pool.wait_ge(res_loaded[t], b * 16 + 16)
                    G.tensor_tensor(xt[:, t, :], y[:, t, :], xt[:, t, :], ALU.add).then_inc(res_added, 1)
            blocks(pool, body)


INPUTS = ["x", "norm_pre", "w_in", "conv_w", "sinks", "w_proj_a", "w_proj_b", "w_out", "norm_post"]


def kernel(**inputs):
    import numpy as np
    import concourse.bacc as bacc
    from concourse.bass_utils import run_bass_kernel_spmd

    nc = bacc.Bacc("TRN2", target_bir_lowering=False, num_devices=1)
    arrays, args = {}, []
    for name in INPUTS:
        a = np.ascontiguousarray(inputs[name])
        arrays[f"{name}_dram"] = a
        args.append(nc.dram_tensor(f"{name}_dram", a.shape, mybir.dt.float32, kind="ExternalInput").ap())
    shape = arrays["x_dram"].shape
    out = nc.dram_tensor("out_dram", shape, mybir.dt.float32, kind="ExternalOutput").ap()
    hybrid_trunk(nc, *args, out)
    r = run_bass_kernel_spmd(nc, [arrays], core_ids=[0])
    return r.results[0]["out_dram"]
```

```python
import concourse.bass as bass
from concourse import mybir
from contextlib import ExitStack


def hybrid_trunk(nc, x, norm_pre, w_in, conv_w, sinks, w_proj_a, w_proj_b, w_out, norm_post, out):
    f32, f32r = mybir.dt.float32, mybir.dt.float32r
    ACT, ALU, AX = mybir.ActivationFunctionType, mybir.AluOpType, mybir.AxisListType

    P = 128
    _, S, D = x.shape
    KT = D // P
    TB = 512
    NB = S // TB
    NT = TB // P
    CHUNK, HD = 64, 64
    NC = TB // CHUNK
    UNIT = 4
    NU = NC // UNIT
    NH = sinks.shape[1]
    NPAIR = NH // 2
    CW = conv_w.shape[1]
    DKV = (w_in.shape[2] - 8 * D) // 2
    SCALE = HD ** -0.5
    WARM = 64
    EPS = 1e-6
    NEG = -1e30
    assert DKV == P and CW == 3 and NPAIR * HD * 2 == D

    C_XA, C_B, C_C, C_ZA, C_Q = 0, D, 2 * D, 3 * D, 4 * D
    C_K = 5 * D
    C_V = C_K + DKV
    C_ZB = C_V + DKV
    C_GA = C_ZB + D
    C_GB = C_GA + D

    J_CONV = 0
    J_CA = J_CONV + 4 * KT
    J_VK = J_CA + 2 * KT
    J_AT = J_VK + 2
    J_CB = J_AT + 2 * NPAIR
    J_OUT = J_CB + 2 * KT
    NJ = J_OUT + KT
    U_CONV, U_CA, U_VK = 0, KT, 2 * KT
    U_AT = U_VK + 1
    U_CB = U_AT + NPAIR
    NU01 = U_CB + KT

    win = w_in[0].rearrange("(t p) n -> p t n", p=P)
    wpa = w_proj_a[0].rearrange("(t p) n -> p t n", p=P)
    wpb = w_proj_b[0].rearrange("(g j d) n -> g d j n", g=2, d=HD)
    wo = w_out[0].rearrange("(t p) n -> p t n", p=P)
    x_tiles = x.rearrange("a (t p) d -> (a t) p d", p=P)
    out_tiles = out.rearrange("a (t p) d -> (a t) p d", p=P)

    with ExitStack() as ctx:
        def sb(name, shape, dt=f32):
            return ctx.enter_context(nc.sbuf_tensor(name, shape, dt))

        def sem(name):
            return ctx.enter_context(nc.semaphore(name))

        h_hi, h_lo = sb("h_hi", [P, KT, TB], f32r), sb("h_lo", [P, KT, TB], f32r)
        u_hi, u_lo = sb("u_hi", [P, KT, TB], f32r), sb("u_lo", [P, KT, TB], f32r)
        m_hi, m_lo = sb("m_hi", [P, KT, TB], f32r), sb("m_lo", [P, KT, TB], f32r)
        pt_hi = m_hi[:, 0:2 * NU, :].rearrange("p (j u) n -> p j u n", u=NU)
        pt_lo = m_lo[:, 0:2 * NU, :].rearrange("p (j u) n -> p j u n", u=NU)
        m_a = sb("m_a", [P, KT, TB])
        xn = m_a[:, :, :].rearrange("p k n -> p (k n)").rearrange("p (t d) -> p t d", t=NT)
        xa_s, th_c, sg_c, gated_c, t_a, t_b, uf_c = (m_a[:, n, :] for n in range(7))
        w_raw = sb("w_raw", [P, 2, KT, P])
        w_hi, w_lo = sb("w_hi", [P, 2, KT, P], f32r), sb("w_lo", [P, 2, KT, P], f32r)
        work = sb("work", [P, KT, TB])
        y = work[:, :, :].rearrange("p k n -> p (k n)").rearrange("p (t d) -> p t d", t=NT)
        th, sg, u_f, p_s = ([work[:, 2 * n + k, :] for k in range(2)] for n in range(4))
        cx = sb("cx", [P, CW - 1 + TB])
        cx_tail = sb("cx_tail", [P, KT, CW - 1])
        keys = sb("keys", [P, 2, 2, CHUNK + TB], f32r)
        v_t = sb("v_t", [P, CHUNK + TB])
        v_hi, v_lo = sb("v_hi", [P, NC, P], f32r), sb("v_lo", [P, NC, P], f32r)
        queries = sb("queries", [P, NC, P], f32r)
        xt = sb("xt", [P, 4, D])
        ident = sb("ident", [P, P])
        gpost = sb("gpost", [P, D])
        gpre = sb("gpre", [P, KT])
        taps = sb("taps", [P, CW, KT])
        sink = sb("sink", [P, NPAIR])
        nsink = sb("nsink", [P, NPAIR])
        mask0 = sb("mask0", [P, 1])
        mx = sb("mx", [P, NU, UNIT])
        negm = sb("negm", [P, NU, UNIT])
        esum = sb("esum", [P, NU, UNIT])
        esink = sb("esink", [P, NU, UNIT])
        den = sb("den", [P, NU, UNIT])
        rden = sb("rden", [P, NU, UNIT])
        ssx = sb("ssx", [P, NT])
        msx = sb("msx", [P, NT])
        rsx = sb("rsx", [P, NT])
        sso = sb("sso", [P, NT, 2])
        mso = sb("mso", [P, NT])
        rso = sb("rso", [P, NT])
        mhalf, eps = sb("mhalf", [P, 1]), sb("eps", [P, 1])

        bank = ctx.enter_context(nc.psum_tensor("bank", [P, 8, TB], f32))
        VAL, TR, SC = 2, 4, 6
        SCORES = (2, 6)
        OUT = ((2, 3, 4, 5), (0, 1, 6, 7))
        assert D == 2 * TB and NT == 4

        raw_loaded = [sem(f"raw_loaded{n}") for n in range(2)]
        whi_ready = sem("whi_ready")
        wlo_ready = [sem(f"wlo_ready{n}") for n in range(2)]
        job_done = sem("job_done")
        drained = [sem(f"drained{n}") for n in range(3)]
        gpre_loaded, consts_loaded, consts_made = map(sem, ("gpre_loaded", "consts_loaded", "consts_made"))
        pool_set, ident_ready = sem("pool_set"), sem("ident_ready")
        x_loaded = [sem(f"x_loaded{n}") for n in range(NT)]
        res_loaded = [sem(f"res_loaded{n}") for n in range(NT)]
        stored = [sem(f"stored{n}") for n in range(NT)]
        xsq_done, xms_done, xrs_ready, xn_ready = map(sem, ("xsq_done", "xms_done", "xrs_ready", "xn_ready"))
        xT_done, hhi_ready, hlo_ready = map(sem, ("xT_done", "hhi_ready", "hlo_ready"))
        tap2_done, tap1_done, tap0_done = map(sem, ("tap2_done", "tap1_done", "tap0_done"))
        tanh_ready, gated_ready = map(sem, ("tanh_ready", "gated_ready"))
        uf_ready, uhi_ready, ulo_ready = map(sem, ("uf_ready", "uhi_ready", "ulo_ready"))
        kvhead_ready, khi_ready, vT_done, vhi_ready, vlo_ready = map(
            sem, ("kvhead_ready", "khi_ready", "vT_done", "vhi_ready", "vlo_ready"))
        tails_moved = sem("tails_moved")
        qhi_ready = sem("qhi_ready")
        scores_done, half_copied, sums_done, masked, max_ready, negm_ready, exp_done = map(
            sem, ("scores_done", "half_copied", "sums_done", "masked", "max_ready", "negm_ready", "exp_done"))
        den_ready, rden_ready, probs_ready = map(sem, ("den_ready", "rden_ready", "probs_ready"))
        pT_done, pthi_ready, ptlo_ready, pv_done = map(sem, ("pT_done", "pthi_ready", "ptlo_ready", "pv_done"))
        msum_ready, mhi_ready, mlo_ready = map(sem, ("msum_ready", "mhi_ready", "mlo_ready"))
        rows_done, rows_out = sem("rows_done"), sem("rows_out")
        osq_done, oms_done, ors_ready, y_scaled, res_added = map(
            sem, ("osq_done", "oms_done", "ors_ready", "y_scaled", "res_added"))

        NORM_AFTER, NORM_BANK = (1, 2, 4, 6), (SC, SC, TR, TR)
        START_BANK = (TR, SC, VAL, TR)

        def columns(at, n):
            return slice(at, at + n) if isinstance(at, int) else bass.ds(at, n)

        def column(tensor, k):
            return tensor[:, columns(k, 1)]

        def column2(tensor, n, k):
            return tensor[:, n, columns(k, 1)]

        def tile(tensor, k):
            return tensor[:, k, :] if isinstance(k, int) else tensor[:, bass.ds(k, 1), :].squeeze(1)

        def f(ap):
            return ap.bitcast(f32)

        def blocks(eng, body):
            with eng.Fori(0, NB - 1) as b:
                body(b, False)
            body(NB - 1, True)

        block = ctx.enter_context(nc.Block())

        @block.sync
        def _(sp):
            def load(slot, parts):
                for dst, src in parts:
                    sp.dma_start(dst, src).then_inc(raw_loaded[slot], 16)

            def cols(slot, src, at):
                h = KT // 2
                return [(w_raw[:, slot, k * h:(k + 1) * h, :], src[:, k * h:(k + 1) * h, bass.ds(at, P)])
                        for k in (1, 0)]

            def head_cols(slot, base, j):
                return [(w_raw[:, slot, :, g * HD:(g + 1) * HD],
                         win[:, :, bass.ds(j * HD + base + g * NPAIR * HD, HD)]) for g in range(2)]

            def head_rows(slot, at):
                return [(w_raw[g * HD:(g + 1) * HD, slot, :, :], wpb[g][:, :, bass.ds(at, P)])
                        for g in (1, 0)]

            def rows(tiles, b, t):
                return tiles[b * NT + t] if isinstance(b, int) else tiles[bass.ds(b * NT + t, 1)].squeeze(0)

            def column(at):
                return at if isinstance(at, int) else sp.snap(at)

            def slot_free(b, j, slot):
                sp.wait_ge(wlo_ready[slot], b * NJ + j - slot)

            def x_rows(b):
                for t in range(NT):
                    sp.dma_start(xt[:, t, :], rows(x_tiles, b, t)).then_inc(x_loaded[t], 16)

            def residual(b, t):
                sp.dma_start(xt[:, t, :], rows(x_tiles, b, t)).then_inc(res_loaded[t], 16)

            def conv(b, i, s0, s1, first=False):
                for s in range(s0, s1):
                    at = column(i * P + (C_XA, C_C, C_ZA, C_B)[s])
                    if not first:
                        slot_free(b, i * 4 + s, s % 2)
                    load(s % 2, cols(s % 2, win, at))

            x_rows(0)
            with nc.allow_non_contiguous_dma(reason="a small constant, once"):
                sp.dma_start(gpre[:, :], norm_pre[0].rearrange("(t p) -> p t", p=P)).then_inc(gpre_loaded, 16)
            conv(0, 0, 0, 2, first=True)
            with nc.allow_non_contiguous_dma(reason="small constants, once"):
                for w in range(CW):
                    sp.dma_start(taps[:, w, :], conv_w[0, w].rearrange("(t p) -> p t", p=P)).then_inc(consts_loaded, 16)
                for a in range(2):
                    for g in range(2):
                        sp.dma_start(sink[a * HD:(a + 1) * HD, :].rearrange("p (i g) -> p i g", g=2)[:, :, g],
                                     sinks.rearrange("o (g i a) -> g a o i", g=2, a=2)[g, a].to_broadcast(
                                         [HD, NPAIR // 2])).then_inc(consts_loaded, 16)
            sp.dma_start(gpost[:, :], norm_post[0:1, :].to_broadcast([P, D])).then_inc(consts_loaded, 16)
            conv(0, 0, 2, 4)
            with sp.Fori(1, KT) as i:
                conv(0, i, 0, 4)

            def body(b, last):
                with sp.Fori(0, KT) as i:
                    for s, (src, c) in enumerate(((win, C_GA), (wpa, 0))):
                        at = column(i * P + c)
                        slot_free(b, i * 2 + J_CA + s, s)
                        load(s, cols(s, src, at))
                for s, c in enumerate((C_V, C_K)):
                    slot_free(b, J_VK + s, s)
                    load(s, cols(s, win, c))
                with sp.Fori(0, NPAIR // 2) as i:
                    for g in range(2):
                        at = column(i * 2 * HD + (C_Q + g * NPAIR * HD))
                        slot_free(b, i * 4 + J_AT + 2 * g, 0)
                        load(0, cols(0, win, at))
                        slot_free(b, i * 4 + J_AT + 2 * g + 1, 1)
                        load(1, head_cols(1, C_ZB + g * HD, i * 2))
                if not last:
                    x_rows(b + 1)
                with sp.Fori(0, KT // 2) as i:
                    at = [column(i * 2 * P + s * P + C_GB) for s in range(2)]
                    at_b = [column(i * 2 * P + s * P) for s in range(2)]
                    for s in range(2):
                        slot_free(b, i * 4 + J_CB + s, s)
                        load(s, cols(s, win, at[s]))
                    for s in range(2):
                        slot_free(b, i * 4 + J_CB + 2 + s, s)
                        load(s, head_rows(s, at_b[s]))
                for c in range(2):
                    with sp.Fori(0, KT // 4) as i:
                        for s in range(2):
                            k = [column(i * 4 + (2 * s + h)) for h in range(2)]
                            slot_free(b, i * 2 + J_OUT + c * (KT // 2) + s, s)
                            load(s, [(w_raw[:, s, h * NT:(h + 1) * NT, :].rearrange("p a n -> p (a n)"),
                                      wo[:, bass.ds(k[h], 1), c * TB:(c + 1) * TB].squeeze(1)) for h in range(2)])
                for t in range(NT):
                    if not last:
                        sp.wait_ge(xn_ready, b * NT + NT + t + 1)
                    residual(b, t)
                if not last:
                    conv(b + 1, 0, 0, 4)
                    with sp.Fori(1, KT - 1) as i:
                        conv(b + 1, i, 0, 4)
                for t in range(NT):
                    sp.wait_ge(res_added, b * NT + t + 2)
                    sp.dma_start(rows(out_tiles, b, t), xt[:, t, :]).then_inc(stored[t], 16)
                if last:
                    for t in range(NT):
                        sp.wait_ge(stored[t], b * 16 + 16)
                else:
                    all_stored = sp.snap(b * 16 + 16)
                    slot_free(b + 1, 4 * (KT - 1), 0)
                    for t in range(NT):
                        sp.wait_ge(stored[t], all_stored)
                    load(0, cols(0, win, (KT - 1) * P + C_XA))
                    conv(b + 1, KT - 1, 1, 4)

            blocks(sp, body)

        @block.tensor
        def _(pe):
            def job(b, j, slot, bk, use, hi, lo, ready=None, beside=None):
                pe.wait_ge(wlo_ready[slot], b * NJ + j + 2 - slot)
                if isinstance(j, int) and j in (0, 1):
                    pe.wait_ge(rows_out, b * 2 * NT + (NT + 1 + j))
                if bk < 2:
                    pe.wait_ge(drained[bk], b * NU01 + use + 1)
                elif bk == 2:
                    pe.wait_ge(drained[2], b * KT + use + 1)
                else:
                    pe.wait_ge(uf_ready, b * 2 * KT + use + 1)
                for k in range(KT):
                    if ready:
                        ready(k)
                    if k == 4 and beside:
                        beside()
                    for n, (w, a) in enumerate(((w_hi, hi), (w_hi, lo), (w_lo, hi))):
                        mm = nc.tensor.matmul(bank[:, bk, :], w[:, slot, k, :], a[:, k, :],
                                              start=(k == 0 and n == 0), stop=(k == KT - 1 and n == 2))
                mm.then_inc(job_done, 1)

            def norm_transposes(b, i, at=SC):
                for s in range(2):
                    for t in range(NT):
                        mm = nc.tensor.transpose(bank[:, at + s, t * P:(t + 1) * P],
                                                 xn[:, t, (i * 2 + s) * P:(i * 2 + s + 1) * P], ident[:, :])
                    mm.then_inc(xT_done, 1)

            def out_job(b, n, last):
                c, kk, slot = n // (KT // 2), n % (KT // 2), n % 2
                pe.wait_ge(wlo_ready[slot], b * NJ + (J_OUT + n + 2 - slot))
                for t in range(NT):
                    if c and kk == 0 and t == 2 and not last:
                        pe.wait_ge(hlo_ready, b * KT + KT + 4)
                    for h in range(2):
                        k = kk * 2 + h
                        if not c and t == 0:
                            pe.wait_ge(mlo_ready, b * KT + k + 1)
                        for i, (m, w) in enumerate(((m_hi, w_hi), (m_hi, w_lo), (m_lo, w_hi))):
                            mm = nc.tensor.matmul(bank[:, OUT[c][t], :], m[:, k, t * P:(t + 1) * P],
                                                  w[:, slot, h * NT:(h + 1) * NT, :].rearrange("p a n -> p (a n)"),
                                                  start=(k == 0 and i == 0), stop=(k == KT - 1 and i == 2))
                    if kk == KT // 2 - 1 and t < NT - 1:
                        mm.then_inc(rows_done, 1)
                mm.then_inc(job_done, 1)

            def probs_transposes(b, j, after_values):
                for u in range(NU):
                    if after_values:
                        if u == 0:
                            pe.wait_ge(uf_ready, b * 2 * KT + j + KT + 1)
                    else:
                        pe.wait_ge(ptlo_ready, (b * NPAIR + j - 1) * NU + u + 1)
                    pe.wait_ge(probs_ready, (b * NPAIR + j) * NU + u + 1)
                    for c in range(UNIT):
                        mm = nc.tensor.transpose(bank[:, TR + u, c * P:(c + 1) * P],
                                                 p_s[u][:, c * P:(c + 1) * P], ident[:, :])
                    mm.then_inc(pT_done, 1)

            def scores(b, j, g):
                pe.wait_ge(drained[0], b * NU01 + j + U_AT + 2)
                for u in range(NU):
                    for c in range(UNIT):
                        n = u * UNIT + c
                        mm = nc.tensor.matmul(bank[:, SCORES[u] + c // 2, c % 2 * 2 * P:(c % 2 + 1) * 2 * P],
                                              queries[:, n, :], keys[:, g, :, n * CHUNK:(n + 2) * CHUNK],
                                              start=True, stop=True)
                    mm.then_inc(scores_done, 1)

            def values(b, i, scored):
                pe.wait_ge(ptlo_ready, (b * NPAIR + i * 2 + 2) * NU)
                pe.wait_ge(uf_ready, b * 2 * KT + i * 2 + KT + 1)
                for n in [*range(UNIT, NC), *range(UNIT)]:
                    u, c = n // UNIT, n % UNIT
                    if n == 0:
                        pe.wait_ge(sums_done, b * (NPAIR * NU) + scored * NU + 1)
                    for m, (v, pt) in enumerate(((v_hi, pt_hi), (v_hi, pt_lo), (v_lo, pt_hi))):
                        mm = nc.tensor.matmul(bank[:, VAL + n // 2, n % 2 * 2 * P:(n % 2 + 1) * 2 * P], v[:, n, :],
                                              pt[:, :, u, c * P:(c + 1) * P], start=(m == 0), stop=(m == 2))
                mm.then_inc(pv_done, 1)

            pe.wait_ge(ident_ready, 1)
            with pe.Fori(0, WARM // 8):
                for _ in range(8):
                    nc.tensor.transpose(bank[:, SC, 0:P], ident[:, :], ident[:, :])
            pe.wait_ge(xn_ready, NT)
            for i in range(KT // 2):
                if i == 3:
                    pe.wait_ge(hlo_ready, 2)
                norm_transposes(0, i, at=START_BANK[i])

            def body(b, last):
                for s in range(4):
                    job(b, s, s % 2, s, U_CONV, h_hi, h_lo,
                        ready=(lambda k: pe.wait_ge(hlo_ready, b * KT + k + 1)) if s == 0 else None)
                with pe.Fori(1, KT) as i:
                    for s in range(4):
                        job(b, i * 4 + s, s % 2, s, i + U_CONV, h_hi, h_lo)
                with pe.Fori(0, KT) as i:
                    job(b, i * 2 + J_CA, 0, 0, i + U_CA, h_hi, h_lo)
                    pe.wait_ge(ulo_ready, b * 2 * KT + KT)
                    job(b, i * 2 + J_CA + 1, 1, 1, i + U_CA, u_hi, u_lo)
                job(b, J_VK, 0, 0, U_VK, h_hi, h_lo)
                job(b, J_VK + 1, 1, 1, U_VK, h_hi, h_lo)

                def query(j):
                    job(b, j * 2 + J_AT, 0, 0, j + U_AT, h_hi, h_lo)

                def z_gate(j, beside=None):
                    job(b, j * 2 + J_AT + 1, 1, 1, j + U_AT, h_hi, h_lo, beside=beside)

                query(0)
                pe.wait_ge(drained[0], b * NU01 + U_VK + 2)
                for u in range(NU):
                    for c in range(UNIT):
                        k0 = (u * UNIT + c) * CHUNK
                        mm = nc.tensor.transpose(bank[:, SC + u, c * P:(c + 1) * P], v_t[:, k0:k0 + 2 * CHUNK], ident[:, :])
                    mm.then_inc(vT_done, 1)
                z_gate(0)
                pe.wait_ge(vlo_ready, b * NU + NU)
                scores(b, 0, 0)
                query(1)
                z_gate(1, lambda: probs_transposes(b, 0, True))
                scores(b, 1, 1)
                with pe.Fori(1, NPAIR // 2) as i:
                    j = i * 2
                    query(j)
                    z_gate(j, lambda: probs_transposes(b, j - 1, False))
                    scores(b, j, 0)
                    values(b, i - 1, j)
                    query(j + 1)
                    z_gate(j + 1, lambda: probs_transposes(b, j, True))
                    scores(b, j + 1, 1)

                def merge(i, first=False, ready=None):
                    job(b, i * 4 + J_CB, 0, 0, i * 2 + U_CB, h_hi, h_lo)
                    job(b, i * 4 + J_CB + 1, 1, 1, i * 2 + U_CB, h_hi, h_lo,
                        beside=(lambda: probs_transposes(b, NPAIR - 1, False)) if first else None)
                    if first:
                        values(b, NPAIR // 2 - 1, NPAIR - 1)
                    job(b, i * 4 + J_CB + 2, 0, 0, i * 2 + U_CB + 1, u_hi, u_lo, ready=ready)
                    job(b, i * 4 + J_CB + 3, 1, 1, i * 2 + U_CB + 1, u_hi, u_lo)

                merge(0, first=True, ready=lambda k: k >= KT - 2 and pe.wait_ge(ulo_ready, b * 2 * KT + KT + k + 1))
                with pe.Fori(1, KT // 2) as i:
                    merge(i)

                for n in range(KT):
                    out_job(b, n, last)
                    if not last and n in NORM_AFTER:
                        i = NORM_AFTER.index(n)
                        if i == 0:
                            pe.wait_ge(xn_ready, b * NT + 2 * NT)
                        elif i == 2:
                            pe.wait_ge(rows_out, b * 2 * NT + 3 * NT)
                        else:
                            pe.wait_ge(hlo_ready, b * KT + KT + i * 2)
                        norm_transposes(b + 1, i, NORM_BANK[i])

            blocks(pe, body)

        @block.scalar
        def _(act):
            def split_hi(b, j, slot, ahead=2):
                n = j + ahead
                act.wait_ge(raw_loaded[slot], b * (NJ * 16) + (n - slot) * 16 + 32)
                if ahead:
                    act.wait_ge(job_done, b * NJ + j + 1)
                nc.scalar.activation(w_hi[:, slot], w_raw[:, slot], ACT.Copy).then_inc(whi_ready, 1)

            def row_squares(b, tiles):
                for t in tiles:
                    act.wait_ge(x_loaded[t], b * 16 + 16)
                    if t == NT - 1:
                        act.wait_ge(xsq_done, b * NT + 1)
                    nc.scalar.activation((queries, v_hi, v_lo, queries)[t][:, :, :].rearrange("p c n -> p (c n)"),
                                         xt[:, t, :], ACT.Square, scale=D ** -0.5, accum_out=ssx[:, t:t + 1]).then_inc(xsq_done, 1)

            def norm_hi(b, i, at=SC):
                for s in range(2):
                    act.wait_ge(xT_done, b * KT + i * 2 + s + 1)
                    nc.scalar.activation(tile(h_hi, i * 2 + s), bank[:, at + s, :], ACT.Copy,
                                         scale=column(gpre, i * 2 + s)).then_inc(hhi_ready, 1)

            def probs_hi(b, j, par):
                for u in range(NU):
                    act.wait_ge(pT_done, (b * NPAIR + j) * NU + u + 1)
                    nc.scalar.activation(pt_hi[:, par, u, :], bank[:, TR + u, :], ACT.Copy).then_inc(pthi_ready, 1)

            def u_high(b, n, k, uf):
                act.wait_ge(uf_ready, b * 2 * KT + n + 2)
                nc.scalar.activation(tile(u_hi, k), uf, ACT.Copy, scale=0.5).then_inc(uhi_ready, 1)

            def exps(b, j, jcol):
                for u in range(NU):
                    act.wait_ge(negm_ready, (b * NPAIR + j) * NU + u + 1)
                    for c in range(UNIT):
                        p = p_s[u][:, c * P:(c + 1) * P]
                        nc.scalar.activation(p, p, ACT.Exp, bias=negm[:, u, c:c + 1], scale=SCALE, accum_out=esum[:, u, c:c + 1])
                    nc.scalar.activation(esink[:, u, :], negm[:, u, :], ACT.Exp,
                                         bias=jcol).then_inc(exp_done, 1)

            row_squares(0, range(NT))
            split_hi(0, 0, 0, ahead=0)
            act.wait_ge(gpre_loaded, 16)
            for i in range(KT // 2):
                norm_hi(0, i, at=START_BANK[i])
                if i == 1:
                    split_hi(0, 1, 1, ahead=0)

            act.wait_ge(consts_loaded, 16 * (CW + 5))

            def body(b, last):
                with act.Fori(0, KT) as i:
                    j = i * 4
                    split_hi(b, j, 0)
                    act.wait_ge(drained[1], b * NU01 + i + 1)
                    nc.scalar.activation(xa_s, bank[:, 0, :], ACT.Copy).then_inc(drained[0], 1)
                    split_hi(b, j + 1, 1)
                    split_hi(b, j + 2, 0)
                    act.wait_ge(drained[2], b * KT + i + 1)
                    nc.scalar.activation(th_c, bank[:, 2, :], ACT.Tanh, scale=0.5).then_inc(tanh_ready, 1)
                    split_hi(b, j + 3, 1)
                    u_high(b, i, i, uf_c)

                with act.Fori(0, KT) as i:
                    j = i * 2 + J_CA
                    split_hi(b, j, 0)
                    act.wait_ge(res_added, b * NT + 1)
                    act.wait_ge(drained[1], b * NU01 + i + U_CA + 1)
                    nc.scalar.activation(th[0], bank[:, 0, :], ACT.Tanh, scale=0.5).then_inc(drained[0], 1)
                    split_hi(b, j + 1, 1)
                act.wait_ge(kvhead_ready, 1)
                for g in range(2):
                    nc.scalar.activation(keys[:, g, :, 0:CHUNK], f(keys[:, g, :, TB:TB + CHUNK]), ACT.Copy)
                nc.scalar.activation(v_t[:, 0:CHUNK], v_t[:, TB:TB + CHUNK], ACT.Copy).then_inc(tails_moved, 1)
                split_hi(b, J_VK, 0)
                act.wait_ge(tails_moved, b + 1)
                nc.scalar.activation(v_t[:, CHUNK:], bank[:, 0, :], ACT.Copy).then_inc(drained[0], 1)
                act.wait_ge(job_done, b * NJ + J_VK + 2)
                for g in range(2):
                    r = slice(g * HD, (g + 1) * HD)
                    for half in range(2):
                        nc.scalar.activation(keys[half * HD:(half + 1) * HD, g, 0, CHUNK:], bank[r, 1, :],
                                             ACT.Copy).then_inc(khi_ready, 1)
                split_hi(b, J_VK + 1, 1)

                def q_high(j):
                    act.wait_ge(job_done, b * NJ + j * 2 + J_AT + 1)
                    q = bank[:, 0, :].rearrange("p (c n) -> p c n", n=CHUNK)
                    for a in range(2):
                        r = slice(a * HD, (a + 1) * HD)
                        nc.scalar.activation(queries[r, :, a * CHUNK:(a + 1) * CHUNK], q[r], ACT.Copy).then_inc(qhi_ready, 1)

                def scores_half(j):
                    for u in range(NU):
                        act.wait_ge(scores_done, (b * NPAIR + j) * NU + u + 1)
                        part = bank[:, SCORES[u]:SCORES[u] + 2, :].rearrange("p a (c h n) -> p (a c) h n", h=2, n=P)
                        nc.scalar.activation(p_s[u].rearrange("p (c n) -> p c n", n=P), part[:, :, 0, :],
                                             ACT.Copy).then_inc(half_copied, 1)

                def z_tanh(j):
                    act.wait_ge(drained[1], b * NU01 + j + U_AT + 1)
                    nc.scalar.activation(th[0], bank[:, 1, :], ACT.Tanh, scale=0.5).then_inc(tanh_ready, 1)

                def u_highs(i):
                    for k in range(2):
                        u_high(b, i * 2 + (KT + k), i * 2 + k, u_f[k])

                q_high(0)
                for u in range(NU):
                    act.wait_ge(vT_done, b * NU + u + 1)
                    nc.scalar.activation(v_hi[:, u * UNIT:(u + 1) * UNIT, :].rearrange("p c n -> p (c n)"),
                                         bank[:, SC + u, :], ACT.Copy).then_inc(vhi_ready, 1)
                split_hi(b, J_AT, 0)
                scores_half(0)
                split_hi(b, J_AT + 1, 1)
                z_tanh(0)
                exps(b, 0, sink[:, 0:1])

                def second(j):
                    q_high(j + 1)
                    split_hi(b, j * 2 + J_AT + 2, 0)
                    probs_hi(b, j, 0)
                    scores_half(j + 1)
                    split_hi(b, j * 2 + J_AT + 3, 1)
                    z_tanh(j + 1)
                    exps(b, j + 1, column(sink, j + 1))

                second(0)
                with act.Fori(1, NPAIR // 2) as i:
                    j = i * 2
                    q_high(j)
                    split_hi(b, j * 2 + J_AT, 0)
                    probs_hi(b, j - 1, 1)
                    scores_half(j)
                    split_hi(b, j * 2 + J_AT + 1, 1)
                    z_tanh(j)
                    exps(b, j, column(sink, j))
                    u_highs(i - 1)
                    second(j)

                def m_high(i, k):
                    act.wait_ge(msum_ready, b * KT + i * 2 + k + 1)
                    nc.scalar.activation(tile(m_hi, i * 2 + k), u_f[k], ACT.Copy, scale=0.5).then_inc(mhi_ready, 1)

                def merge(i, first=False):
                    j = i * 4 + J_CB
                    split_hi(b, j, 0)
                    act.wait_ge(drained[1], b * NU01 + i * 2 + U_CB + 1)
                    nc.scalar.activation(th[0], bank[:, 0, :], ACT.Tanh, scale=0.5).then_inc(drained[0], 1)
                    if first:
                        probs_hi(b, NPAIR - 1, 1)
                    split_hi(b, j + 1, 1)
                    nc.scalar.activation(th[1], bank[:, 1, :], ACT.Tanh, scale=0.5).then_inc(drained[1], 1)
                    if first:
                        u_highs(NPAIR // 2 - 1)
                    split_hi(b, j + 2, 0)
                    m_high(i, 0)
                    split_hi(b, j + 3, 1)
                    m_high(i, 1)

                merge(0, first=True)
                if not last:
                    row_squares(b + 1, range(NT // 2))
                with act.Fori(1, KT // 2) as i:
                    merge(i)
                if not last:
                    row_squares(b + 1, range(NT // 2, NT))

                def out_squares(c, t):
                    if t < NT - 1:
                        act.wait_ge(rows_done, (b * 2 + c) * (NT - 1) + t + 1)
                    else:
                        act.wait_ge(job_done, b * NJ + J_OUT + (c + 1) * (KT // 2))
                    nc.scalar.activation(u_lo[:, c * NT + t, :], bank[:, OUT[c][t], :], ACT.Square, scale=D ** -0.5,
                                         accum_out=sso[:, t, c:c + 1]).then_inc(osq_done, 1)

                for n in range(KT):
                    c = n // (KT // 2)
                    half_ends = n % (KT // 2) == KT // 2 - 1
                    if half_ends:
                        for t in range(NT - 1):
                            out_squares(c, t)
                    if not last or n < KT - 2:
                        split_hi(b, J_OUT + n, n % 2)
                    if half_ends:
                        out_squares(c, NT - 1)
                    if not last and n in NORM_AFTER:
                        i = NORM_AFTER.index(n)
                        norm_hi(b + 1, i, NORM_BANK[i])

            blocks(act, body)

        @block.vector
        def _(dve):
            V = nc.vector

            def split_lo(b, j, slot, ahead=2):
                n = j + ahead
                dve.wait_ge(whi_ready, b * NJ + n + 1)
                V.tensor_tensor(w_lo[:, slot], w_raw[:, slot], f(w_hi[:, slot]), ALU.subtract).then_inc(wlo_ready[slot], 2)

            def row_scale(b):
                for t in range(NT):
                    dve.wait_ge(xrs_ready, b * NT + t + 1)
                    V.tensor_scalar(xn[:, t, :], xt[:, t, :], rsx[:, t:t + 1], None, ALU.mult).then_inc(xn_ready, 1)

            def norm_lo(b, i, at=SC):
                for s in range(2):
                    dve.wait_ge(hhi_ready, b * KT + i * 2 + s + 1)
                    k = i * 2 + s
                    V.scalar_tensor_tensor(tile(h_lo, k), bank[:, at + s, :], column(gpre, k),
                                           f(tile(h_hi, k)), ALU.mult, ALU.subtract).then_inc(hlo_ready, 1)

            def u_low(b, n, k, uf):
                dve.wait_ge(uhi_ready, b * 2 * KT + n + 1)
                V.scalar_tensor_tensor(tile(u_lo, k), uf, 0.5, f(tile(u_hi, k)), ALU.mult,
                                       ALU.subtract).then_inc(ulo_ready, 1)

            V.memset(cx_tail[:, :, :], 0.0).then_inc(drained[0], 1)
            V.memset(keys[:, :, :, TB:TB + CHUNK].bitcast(mybir.dt.uint32), 0).then_inc(drained[1], 1)
            V.memset(mask0[:, :], NEG).then_inc(drained[2], 1)
            V.memset(v_t[:, TB:TB + CHUNK], 0.0).then_inc(kvhead_ready, 1)
            V.memset(sso[:, :, :], 0.0).then_inc(uf_ready, 1)
            V.memset(den[:, :, :], 0.0).then_inc(rows_out, 2 * NT)
            row_scale(0)
            split_lo(0, 0, 0, ahead=0)
            dve.wait_ge(gpre_loaded, 16)
            for i in range(KT // 2):
                norm_lo(0, i, at=START_BANK[i])
            dve.wait_ge(consts_loaded, 16 * (CW + 5))
            V.tensor_scalar(nsink[:, :], sink[:, :], -1.0, None, ALU.mult).then_inc(consts_made, 1)
            dve.wait_ge(consts_made, 1)

            def body(b, last):
                with dve.Fori(0, KT) as i:
                    j = i * 4
                    n = b * KT + i
                    split_lo(b, j, 0)
                    tail = tile(cx_tail, i)
                    V.tensor_copy(cx[:, 0:CW - 1], tail)
                    dve.wait_ge(drained[0], b * NU01 + i + 2)
                    dve.wait_ge(job_done, b * NJ + j + 2)
                    V.tensor_tensor(cx[:, CW - 1:], bank[:, 1, :], xa_s, ALU.mult).then_inc(drained[1], 1)
                    split_lo(b, j + 1, 1)
                    dve.wait_ge(drained[1], b * NU01 + i + 2)
                    V.tensor_scalar(t_a, cx[:, 2:2 + TB], column2(taps, 2, i), None, ALU.mult).then_inc(tap2_done, 1)
                    V.tensor_copy(tail, cx[:, TB:])
                    dve.wait_ge(tap2_done, n + 1)
                    V.scalar_tensor_tensor(t_b, cx[:, 1:1 + TB], column2(taps, 1, i), t_a,
                                           ALU.mult, ALU.add).then_inc(tap1_done, 1)
                    dve.wait_ge(tap1_done, n + 1)
                    V.scalar_tensor_tensor(t_a, cx[:, 0:TB], column2(taps, 0, i), t_b,
                                           ALU.mult, ALU.add).then_inc(tap0_done, 1)
                    split_lo(b, j + 2, 0)
                    dve.wait_ge(tanh_ready, b * (KT + NPAIR) + i + 1)
                    V.scalar_tensor_tensor(sg_c, th_c, 1.0, bank[:, 2, :], ALU.add, ALU.mult).then_inc(drained[2], 1)
                    dve.wait_ge(drained[2], n + 2)
                    dve.wait_ge(tap0_done, n + 1)
                    V.tensor_tensor(gated_c, sg_c, t_a, ALU.mult).then_inc(gated_ready, 1)
                    dve.wait_ge(job_done, b * NJ + j + 4)
                    dve.wait_ge(gated_ready, n + 1)
                    V.tensor_tensor(uf_c, bank[:, 3, :], gated_c, ALU.mult).then_inc(uf_ready, 1)
                    split_lo(b, j + 3, 1)
                    u_low(b, i, i, uf_c)
                with dve.Fori(0, KT) as i:
                    j = i * 2 + J_CA
                    split_lo(b, j, 0)
                    dve.wait_ge(drained[0], b * NU01 + i + U_CA + 2)
                    dve.wait_ge(job_done, b * NJ + j + 2)
                    V.scalar_tensor_tensor(tile(m_a, i), th[0], 1.0, bank[:, 1, :], ALU.add, ALU.mult).then_inc(drained[1], 1)
                    split_lo(b, j + 1, 1)
                split_lo(b, J_VK, 0)
                dve.wait_ge(khi_ready, b * 4 + 4)
                for g in range(2):
                    r = slice(g * HD, (g + 1) * HD)
                    for half in range(2):
                        i_ = V.tensor_tensor(keys[half * HD:(half + 1) * HD, g, 1, CHUNK:], bank[r, 1, :],
                                             f(keys[r, g, 0, CHUNK:]), ALU.subtract)
                i_.then_inc(drained[1], 1)
                split_lo(b, J_VK + 1, 1)

                def q_low(j):
                    dve.wait_ge(qhi_ready, (b * NPAIR + j) * 2 + 2)
                    q = bank[:, 0, :].rearrange("p (c n) -> p c n", n=CHUNK)
                    for a in range(2):
                        r, n = slice(a * HD, (a + 1) * HD), slice(a * CHUNK, (a + 1) * CHUNK)
                        i_ = V.tensor_tensor(queries[(1 - a) * HD:(2 - a) * HD, :, n], q[r], f(queries[r, :, n]),
                                             ALU.subtract)
                    i_.then_inc(drained[0], 1)

                def maxima(j):
                    n = (b * NPAIR + j) * NU
                    for u in range(NU):
                        part = bank[:, SCORES[u]:SCORES[u] + 2, :].rearrange("p a (c h n) -> p (a c) h n", h=2, n=P)
                        p = p_s[u].rearrange("p (c n) -> p c n", n=P)
                        dve.wait_ge(half_copied, n + u + 1)
                        V.tensor_tensor(p, part[:, :, 1, :], p, ALU.add).then_inc(sums_done, 1)
                        dve.wait_ge(sums_done, n + u + 1)
                        if u == 0:
                            V.tensor_scalar(p_s[0][:, 0:CHUNK], p_s[0][:, 0:CHUNK], mask0[:, :], None,
                                            ALU.add).then_inc(masked, 1)
                            dve.wait_ge(masked, b * NPAIR + j + 1)
                        V.tensor_reduce(mx[:, u, :], p, AX.X, ALU.max).then_inc(max_ready, 1)
                        dve.wait_ge(max_ready, n + u + 1)
                        V.tensor_scalar(negm[:, u, :], mx[:, u, :], -SCALE, column(nsink, j), ALU.mult,
                                        ALU.min).then_inc(negm_ready, 1)

                def normalise(j):
                    n = (b * NPAIR + j) * NU
                    for u in range(NU):
                        dve.wait_ge(exp_done, n + u + 1)
                        V.tensor_tensor(den[:, u, :], esum[:, u, :], esink[:, u, :], ALU.add).then_inc(den_ready, 1)
                        dve.wait_ge(den_ready, n + u + 1)
                        V.reciprocal(rden[:, u, :], den[:, u, :]).then_inc(rden_ready, 1)
                        dve.wait_ge(rden_ready, n + u + 1)
                        pr = p_s[u].rearrange("p (c n) -> p c n", n=P)
                        V.tensor_tensor(pr, pr, rden[:, u, :].unsqueeze(2).to_broadcast([P, UNIT, P]),
                                        ALU.mult).then_inc(probs_ready, 1)

                def gate(j, k):
                    dve.wait_ge(tanh_ready, b * (KT + NPAIR) + KT + j + 1)
                    V.scalar_tensor_tensor(sg[k], th[0], 1.0, bank[:, 1, :], ALU.add, ALU.mult).then_inc(drained[1], 1)

                def probs_lo(j, par):
                    for u in range(NU):
                        dve.wait_ge(pthi_ready, (b * NPAIR + j) * NU + u + 1)
                        V.tensor_tensor(pt_lo[:, par, u, :], bank[:, TR + u, :], f(pt_hi[:, par, u, :]),
                                        ALU.subtract).then_inc(ptlo_ready, 1)

                def attended(i):
                    dve.wait_ge(pv_done, b * (NPAIR // 2) + i + 1)
                    dve.wait_ge(ulo_ready, b * 2 * KT + i * 2 + KT)
                    dve.wait_ge(drained[1], b * NU01 + i * 2 + U_AT + 3)
                    for k in range(2):
                        for g in range(2):
                            r = slice(g * HD, (g + 1) * HD)
                            i_ = V.tensor_tensor(
                                u_f[k][r].rearrange("p (c n) -> p c n", n=CHUNK),
                                bank[r, VAL:VAL + 4, :].rearrange("p a (c j n) -> p (a c) j n", j=2, n=P)
                                [:, :, g, k * CHUNK:(k + 1) * CHUNK],
                                sg[k][r].rearrange("p (c n) -> p c n", n=CHUNK), ALU.mult)
                        i_.then_inc(uf_ready, 1)

                def u_lows(i):
                    for k in range(2):
                        u_low(b, i * 2 + (KT + k), i * 2 + k, u_f[k])

                q_low(0)
                for u in range(NU):
                    dve.wait_ge(vhi_ready, b * NU + u + 1)
                    vs = slice(u * UNIT, (u + 1) * UNIT)
                    V.tensor_tensor(v_lo[:, vs, :].rearrange("p c n -> p (c n)"), bank[:, SC + u, :],
                                    f(v_hi[:, vs, :]).rearrange("p c n -> p (c n)"), ALU.subtract).then_inc(vlo_ready, 1)
                split_lo(b, J_AT, 0)
                maxima(0)
                gate(0, 0)
                normalise(0)

                def second(j):
                    q_low(j + 1)
                    split_lo(b, j * 2 + J_AT + 2, 0)
                    probs_lo(j, 0)
                    maxima(j + 1)
                    gate(j + 1, 1)
                    normalise(j + 1)

                second(0)
                with dve.Fori(1, NPAIR // 2) as i:
                    j = i * 2
                    q_low(j)
                    split_lo(b, j * 2 + J_AT, 0)
                    probs_lo(j - 1, 1)
                    maxima(j)
                    attended(i - 1)
                    dve.wait_ge(uf_ready, b * 2 * KT + KT + j + 1)
                    gate(j, 0)
                    normalise(j)
                    u_lows(i - 1)
                    second(j)
                V.memset(mask0[:, :], 0.0)

                def merge_tile(i, k):
                    n = b * KT + i * 2 + k
                    dve.wait_ge(job_done, b * NJ + i * 4 + (J_CB + 3 + k))
                    dve.wait_ge(drained[k], b * NU01 + i * 2 + U_CB + 2)
                    V.scalar_tensor_tensor(sg[k], th[k], 1.0, bank[:, k, :], ALU.add, ALU.mult).then_inc(drained[k], 1)
                    dve.wait_ge(drained[k], b * NU01 + i * 2 + U_CB + 3)
                    V.tensor_tensor(u_f[k], sg[k], tile(m_a, i * 2 + k), ALU.add).then_inc(msum_ready, 1)

                def m_low(i, k):
                    dve.wait_ge(mhi_ready, b * KT + i * 2 + k + 1)
                    V.scalar_tensor_tensor(tile(m_lo, i * 2 + k), u_f[k], 0.5, f(tile(m_hi, i * 2 + k)), ALU.mult,
                                           ALU.subtract).then_inc(mlo_ready, 1)

                def merge(i, first=False):
                    j = i * 4 + J_CB
                    split_lo(b, j, 0)
                    if first:
                        probs_lo(NPAIR - 1, 1)
                    split_lo(b, j + 1, 1)
                    if first:
                        attended(NPAIR // 2 - 1)
                        u_lows(NPAIR // 2 - 1)
                    merge_tile(i, 0)
                    split_lo(b, j + 2, 0)
                    m_low(i, 0)
                    merge_tile(i, 1)
                    m_low(i, 1)
                    split_lo(b, j + 3, 1)

                merge(0, first=True)
                with dve.Fori(1, KT // 2) as i:
                    merge(i)
                if not last:
                    row_scale(b + 1)

                def out_scale(c, t):
                    dve.wait_ge(osq_done, b * 2 * NT + c * NT + t + 1)
                    V.tensor_tensor(y[:, t, c * TB:(c + 1) * TB], bank[:, OUT[c][t], :],
                                    gpost[:, c * TB:(c + 1) * TB], ALU.mult).then_inc(rows_out, 1)

                def out_norm(t):
                    dve.wait_ge(rows_out, b * 2 * NT + 3 * NT + t + 1)
                    dve.wait_ge(ors_ready, b * NT + t + 1)
                    dve.wait_ge(res_loaded[t], b * 16 + 16)
                    V.scalar_tensor_tensor(xt[:, t, :], y[:, t, :], rso[:, t:t + 1], xt[:, t, :], ALU.mult,
                                           ALU.add).then_inc(res_added, 1)

                for n in range(KT):
                    c = n // (KT // 2)
                    half_ends = n % (KT // 2) == KT // 2 - 1
                    if half_ends:
                        for t in range(NT - 1):
                            out_scale(c, t)
                            if last and c and t:
                                out_norm(t - 1)
                    if not last or n < KT - 2:
                        split_lo(b, J_OUT + n, n % 2)
                    if half_ends:
                        out_scale(c, NT - 1)
                    if not last and n in NORM_AFTER:
                        i = NORM_AFTER.index(n)
                        norm_lo(b + 1, i, NORM_BANK[i])
                if last:
                    for t in (NT - 2, NT - 1):
                        out_norm(t)

            blocks(dve, body)

        @block.gpsimd
        def _(pool):
            G = nc.gpsimd
            G.memset(ident[:, :], 0.0).then_inc(pool_set, 1)
            G.memset(mhalf[:, :], -0.5).then_inc(pool_set, 1)
            G.memset(eps[:, :], EPS).then_inc(pool_set, 1)
            G.memset(mso[:, :], 0.0).then_inc(res_added, 1)
            pool.wait_ge(pool_set, 3)
            G.affine_select(out=ident[:, :], in_=ident[:, :], compare_op=ALU.not_equal, fill=1.0, base=0,
                            pattern=[[-1, P]], channel_multiplier=1).then_inc(ident_ready, 1)

            def power(ms, rs, ready):
                G.tensor_tensor(rs, ms, mhalf[:, :], ALU.pow).then_inc(ready, 1)

            def slot1_lo(splits):
                pool.wait_ge(whi_ready, splits)
                G.tensor_tensor(w_lo[:, 1], w_raw[:, 1], f(w_hi[:, 1]), ALU.subtract).then_inc(wlo_ready[1], 2)

            def row_rstd(b):
                for t in range(NT):
                    c = slice(t, t + 1)
                    pool.wait_ge(xsq_done, b * NT + t + 1)
                    G.tensor_tensor(msx[:, c], ssx[:, c], eps[:, :], ALU.add).then_inc(xms_done, 1)
                    pool.wait_ge(xms_done, b * NT + t + 1)
                    power(msx[:, c], rsx[:, c], xrs_ready)

            row_rstd(0)
            slot1_lo(2)

            def body(b, last):
                with pool.Fori(0, NPAIR) as j:
                    slot1_lo(b * NJ + j * 2 + (J_AT + 4))
                if not last:
                    row_rstd(b + 1)
                for t in range(NT):
                    c, n = slice(t, t + 1), b * NT + t
                    pool.wait_ge(osq_done, b * 2 * NT + NT + t + 1)
                    G.tensor_tensor(mso[:, c], sso[:, t, 0:1], sso[:, t, 1:2], ALU.add).then_inc(oms_done, 1)
                    pool.wait_ge(oms_done, n * 2 + 1)
                    G.tensor_tensor(mso[:, c], mso[:, c], eps[:, :], ALU.add).then_inc(oms_done, 1)
                    pool.wait_ge(oms_done, n * 2 + 2)
                    power(mso[:, c], rso[:, c], ors_ready)
                    if not last:
                        pool.wait_ge(ors_ready, n + 1)
                        pool.wait_ge(rows_out, b * 2 * NT + 3 * NT + t + 1)
                        G.tensor_tensor(y[:, t, :], y[:, t, :], rso[:, c].to_broadcast([P, D]), ALU.mult).then_inc(y_scaled, 1)
                        pool.wait_ge(y_scaled, n + 1)
                        pool.wait_ge(res_loaded[t], b * 16 + 16)
                        G.tensor_tensor(xt[:, t, :], y[:, t, :], xt[:, t, :], ALU.add).then_inc(res_added, 1)

            blocks(pool, body)


INPUTS = ["x", "norm_pre", "w_in", "conv_w", "sinks", "w_proj_a", "w_proj_b", "w_out", "norm_post"]


def kernel(**inputs):
    import numpy as np
    import concourse.bacc as bacc
    from concourse.bass_utils import run_bass_kernel_spmd

    nc = bacc.Bacc("TRN2", target_bir_lowering=False, num_devices=1)
    arrays, args = {}, []
    for name in INPUTS:
        a = np.ascontiguousarray(inputs[name])
        arrays[f"{name}_dram"] = a
        args.append(nc.dram_tensor(f"{name}_dram", a.shape, mybir.dt.float32, kind="ExternalInput").ap())
    shape = arrays["x_dram"].shape
    out = nc.dram_tensor("out_dram", shape, mybir.dt.float32, kind="ExternalOutput").ap()
    hybrid_trunk(nc, *args, out)
    r = run_bass_kernel_spmd(nc, [arrays], core_ids=[0])
    return r.results[0]["out_dram"]
```
